# Optimizing a Trainium2 kernel written in Bass

```python
import math
import jax, jax.numpy as jnp
from jax import lax
import numpy as np

D_MODEL = 1024
BATCH = 1
SEQ = 512
DEPTH = 1
DEC_BATCH = 8
DEC_SEQ = 8
PAST_LEN = 2048
PAGE_SIZE = 128

M_HEADS = 4
M_HEAD_DIM = 128
M_WIDTH = M_HEADS * M_HEAD_DIM
M_CHUNK = 64
CONV_WIDTH = 4
QK_WIDTH = 2 * M_WIDTH
A_HEADS = 4
A_HEAD_DIM = 128
A_GROUP_WIDTH = A_HEADS * A_HEAD_DIM
WINDOWS = (128, 512, 2048)
DILATIONS = (1, 4, 16)
N_GROUPS = 3
A_OUT_WIDTH = A_GROUP_WIDTH
IN_SPLITS = (QK_WIDTH, M_WIDTH, M_WIDTH, M_HEADS, M_HEADS) + (A_GROUP_WIDTH,) * (3 * N_GROUPS) + (D_MODEL, D_MODEL)
D_IN = sum(IN_SPLITS)
P_HEADS = 8
P_QDIM = 256
P_HALF = P_QDIM // 2
P_NKEYS = 128
P_EXPERTS = P_NKEYS * P_NKEYS
P_TOPK = 16
P_TOKEN_BLOCK = 256
RMS_EPS = 1e-6

kernel_name = 'hybrid_mlstm_dilated_attn_peer_step'

def _rmsnorm(x, g):
    x32 = x.astype(jnp.float32)
    y = x32 * lax.rsqrt(jnp.mean(x32 * x32, axis=-1, keepdims=True) + RMS_EPS)
    return (y * g.astype(jnp.float32)).astype(x.dtype)

def _softmax_lse(s):
    m = jnp.max(s, axis=-1, keepdims=True)
    e = jnp.exp(s - m)
    l = jnp.sum(e, axis=-1, keepdims=True)
    return e / l, (m + jnp.log(l))[..., 0]

def _causal_conv(u, state, w, b):
    L = u.shape[1]
    uu = jnp.concatenate([state.astype(u.dtype), u], axis=1)
    out = b + w[0] * uu[:, 0:L]
    for j in range(1, CONV_WIDTH):
        out = out + w[j] * uu[:, j:j + L]
    return out, uu[:, L:]

def _mlstm_chunkwise(q, k, v, ipre, logf, C0, n0, m0):
    B, H, L, _ = q.shape
    lc = math.gcd(L, M_CHUNK)
    nc = L // lc

    def chunks(t):
        return jnp.moveaxis(t.reshape(t.shape[:2] + (nc, lc) + t.shape[3:]), 2, 0)

    causal = jnp.tril(jnp.ones((lc, lc), dtype=bool))

    def step(carry, inp):
        C, n, m = carry
        qc, kc, vc, ic, fc = inp
        b = jnp.cumsum(fc, axis=-1)
        dmat = b[..., :, None] - b[..., None, :] + ic[..., None, :]
        dmat = jnp.where(causal, dmat, -jnp.inf)
        inter = b + m[..., None]
        mt = jnp.maximum(inter, jnp.max(dmat, axis=-1))
        w_in = jnp.exp(dmat - mt[..., None])
        w_prev = jnp.exp(inter - mt)
        s = jnp.einsum('bhtd,bhsd->bhts', qc, kc) * w_in
        num = jnp.einsum('bhts,bhsv->bhtv', s, vc) + w_prev[..., None] * jnp.einsum('bhtk,bhkv->bhtv', qc, C)
        den = jnp.sum(s, axis=-1) + w_prev * jnp.einsum('bhtk,bhk->bht', qc, n)
        h = num / jnp.maximum(jnp.abs(den), jnp.exp(-mt))[..., None]
        m_new = mt[..., -1]
        w_end = jnp.exp(b[..., -1:] - b + ic - m_new[..., None])
        decay = jnp.exp(b[..., -1] + m - m_new)
        C_new = decay[..., None, None] * C + jnp.einsum('bhs,bhsk,bhsv->bhkv', w_end, kc, vc)
        n_new = decay[..., None] * n + jnp.einsum('bhs,bhsk->bhk', w_end, kc)
        return (C_new, n_new, m_new), h

    (C, n, m), hs = lax.scan(step, (C0, n0, m0),
                             (chunks(q), chunks(k), chunks(v), chunks(ipre), chunks(logf)))
    h = jnp.moveaxis(hs, 0, 2).reshape(B, H, L, v.shape[-1])
    return h, C, n, m

def _band_dilated_attn(q, k, v, window, dil):
    B, S, H, hd = q.shape
    nw = window // dil
    ls = S // dil
    blk = min(nw, ls)
    nb = -(-ls // blk)
    lp = nb * blk

    def sub(t, front):
        t = t.astype(jnp.float32).reshape(B, ls, dil, H, hd)
        return jnp.pad(t, ((0, 0), (front, lp - ls), (0, 0), (0, 0), (0, 0)))

    qs = sub(q, 0).reshape(B, nb, blk, dil, H, hd)
    ks = sub(k, blk).reshape(B, nb + 1, blk, dil, H, hd)
    vs = sub(v, blk).reshape(B, nb + 1, blk, dil, H, hd)
    kb = jnp.concatenate([ks[:, :-1], ks[:, 1:]], axis=2)
    vb = jnp.concatenate([vs[:, :-1], vs[:, 1:]], axis=2)
    s = jnp.einsum('bnqrhd,bnkrhd->bnrhqk', qs, kb) * (hd ** -0.5)
    qi = jnp.arange(blk)[:, None] + blk
    ki = jnp.arange(2 * blk)[None, :]
    dist = qi - ki
    kpos = jnp.arange(nb)[:, None, None] * blk + ki[None] - blk
    mask = (dist >= 0) & (dist <= nw) & (kpos >= 0)
    s = jnp.where(mask[None, :, None, None], s, -jnp.inf)
    p, lse = _softmax_lse(s)
    o = jnp.einsum('bnrhqk,bnkrhd->bnqrhd', p, vb)
    o = o.reshape(B, lp, dil, H, hd)[:, :ls].reshape(B, S, H, hd)
    lse = lse.transpose(0, 1, 4, 2, 3).reshape(B, lp, dil, H)[:, :ls].reshape(B, S, H)
    return o, lse

def _gathered_dilated_attn(q, k, v, buf, window, dil):
    T = q.shape[1]
    Wb = buf.shape[1]
    nw = window // dil
    ek = jnp.concatenate([buf[:, :, 0].astype(k.dtype), k], axis=1)
    ev = jnp.concatenate([buf[:, :, 1].astype(v.dtype), v], axis=1)
    idx = Wb + jnp.arange(T)[:, None] - dil * jnp.arange(nw + 1)[None, :]
    valid = idx >= 0
    idx = jnp.maximum(idx, 0)
    kg = ek[:, idx].astype(jnp.float32)
    vg = ev[:, idx].astype(jnp.float32)
    s = jnp.einsum('bthd,btjhd->bthj', q.astype(jnp.float32), kg) * (q.shape[-1] ** -0.5)
    s = jnp.where(valid[None, :, None, :], s, -jnp.inf)
    p, lse = _softmax_lse(s)
    o = jnp.einsum('bthj,btjhd->bthd', p, vg)
    new_buf = jnp.stack([ek[:, -Wb:], ev[:, -Wb:]], axis=2)
    return o, lse, new_buf

def _peer(h, wq, k1, k2, u, v):
    T = h.shape[0]
    blk = math.gcd(T, P_TOKEN_BLOCK)

    def one_block(hb):
        q = (hb @ wq).reshape(blk, P_HEADS, P_QDIM).astype(jnp.float32)
        s1 = jnp.einsum('thd,nd->thn', q[..., :P_HALF], k1.astype(jnp.float32))
        s2 = jnp.einsum('thd,nd->thn', q[..., P_HALF:], k2.astype(jnp.float32))
        v1, i1 = lax.top_k(s1, P_TOPK)
        v2, i2 = lax.top_k(s2, P_TOPK)
        cand = (v1[..., :, None] + v2[..., None, :]).reshape(blk, P_HEADS, P_TOPK * P_TOPK)
        cidx = (i1[..., :, None] * P_NKEYS + i2[..., None, :]).reshape(blk, P_HEADS, P_TOPK * P_TOPK)
        sc, pos = lax.top_k(cand, P_TOPK)
        eidx = jnp.take_along_axis(cidx, pos, axis=-1)
        g = jax.nn.softmax(sc, axis=-1)
        act = jax.nn.gelu(jnp.einsum('td,thkd->thk', hb, u[eidx]).astype(jnp.float32), approximate=False)
        return jnp.einsum('thk,thkd->td', (g * act).astype(hb.dtype), v[eidx])

    out = lax.map(one_block, h.reshape(T // blk, blk, h.shape[-1]))
    return out.reshape(T, h.shape[-1])

def _layer(x, c, state, prm):
    B, L, _ = x.shape
    dt = x.dtype
    f32 = jnp.float32
    prompt = state is None
    if prompt:
        bufs = (None,) * N_GROUPS
        C0 = jnp.zeros((B, M_HEADS, M_HEAD_DIM, M_HEAD_DIM), f32)
        n0 = jnp.zeros((B, M_HEADS, M_HEAD_DIM), f32)
        m0 = jnp.zeros((B, M_HEADS), f32)
        conv_s = jnp.zeros((B, CONV_WIDTH - 1, QK_WIDTH), dt)
    else:
        bufs = state[:N_GROUPS]
        C0 = state[3].astype(f32)
        n0 = state[4].astype(f32)
        m0 = state[5].astype(f32)
        conv_s = state[6]

    mod = (jax.nn.silu(c) @ prm['w_ada'] + prm['b_ada'])[:, None, :]
    sh1, sc1, ga1, sh2, sc2, ga2 = jnp.split(mod, 6, axis=-1)

    h = _rmsnorm(x, prm['g_pre1']) * (1 + sc1) + sh1
    split_points = np.cumsum(IN_SPLITS)[:-1].tolist()
    parts = jnp.split(h @ prm['w_in'], split_points, axis=-1)

    qk, conv_new = _causal_conv(parts[0], conv_s, prm['conv_w'], prm['conv_b'])
    qk = jax.nn.silu(qk)

    def heads(t):
        return t.reshape(B, L, M_HEADS, M_HEAD_DIM).transpose(0, 2, 1, 3).astype(f32)

    qm = heads(qk[..., :M_WIDTH])
    km = heads(qk[..., M_WIDTH:]) * (M_HEAD_DIM ** -0.5)
    vm = heads(parts[1])
    ipre = (parts[3] + prm['b_igate']).astype(f32).transpose(0, 2, 1)
    logf = jax.nn.log_sigmoid((parts[4] + prm['b_fgate']).astype(f32)).transpose(0, 2, 1)
    hm, C1, n1, m1 = _mlstm_chunkwise(qm, km, vm, ipre, logf, C0, n0, m0)
    hm = hm.transpose(0, 2, 1, 3) * jax.nn.sigmoid(parts[2].astype(f32)).reshape(B, L, M_HEADS, M_HEAD_DIM)
    hm = hm * lax.rsqrt(jnp.mean(hm * hm, axis=-1, keepdims=True) + RMS_EPS)
    hm = (hm.reshape(B, L, M_WIDTH) * prm['mh_norm_g'].astype(f32)).astype(dt)
    branch_a = hm @ prm['w_a']

    outs, lses, new_bufs = [], [], []
    for g in range(N_GROUPS):
        qa, ka, va = (t.reshape(B, L, A_HEADS, A_HEAD_DIM) for t in parts[5 + 3 * g:8 + 3 * g])
        if prompt:
            o, lse = _band_dilated_attn(qa, ka, va, WINDOWS[g], DILATIONS[g])
            keep = min(WINDOWS[g], L)
            nbuf = jnp.stack([ka[:, L - keep:], va[:, L - keep:]], axis=2)
        else:
            o, lse, nbuf = _gathered_dilated_attn(qa, ka, va, bufs[g], WINDOWS[g], DILATIONS[g])
        outs.append(o)
        lses.append(lse)
        new_bufs.append(nbuf)
    wgt = jax.nn.softmax(jnp.stack(lses), axis=0)
    oa = jnp.einsum('gblh,gblhd->blhd', wgt, jnp.stack(outs)).reshape(B, L, A_OUT_WIDTH).astype(dt)
    branch_b = oa @ prm['w_b']

    merged = jax.nn.sigmoid(parts[14]) * branch_a + jax.nn.sigmoid(parts[15]) * branch_b
    x = x + ga1 * _rmsnorm(merged @ prm['w_out'], prm['g_post1'])

    h2 = _rmsnorm(x, prm['g_pre2']) * (1 + sc2) + sh2
    f = _peer(h2.reshape(B * L, D_MODEL), prm['peer_wq'], prm['peer_k1'], prm['peer_k2'],
              prm['peer_u'], prm['peer_v']).reshape(B, L, D_MODEL)
    x = x + ga2 * _rmsnorm(f, prm['g_post2'])
    return x, (new_bufs[0], new_bufs[1], new_bufs[2], C1, n1, m1, conv_new)

def setup_inputs(seed: int = 0) -> dict:
    key = jax.random.key(seed)
    ks = jax.random.split(key, 40)
    f32 = jnp.float32

    def nrm(k, shape, scale):
        return jax.random.normal(k, shape, f32) * scale

    def gain(k, shape):
        return 1.0 + 0.02 * jax.random.normal(k, shape, f32)

    D = D_MODEL
    inp = {}
    inp['x_prompt'] = nrm(ks[0], (BATCH, SEQ, D), 1.0)
    inp['x_sample'] = nrm(ks[1], (DEC_BATCH, DEC_SEQ, D), 1.0)
    for g in range(N_GROUPS):
        inp['cache_win%d_kv' % g] = nrm(ks[2 + g], (DEPTH, DEC_BATCH, min(WINDOWS[g], PAST_LEN), 2, A_HEADS, A_HEAD_DIM), 1.0)
    inp['state_mlstm_C'] = nrm(ks[5], (DEPTH, DEC_BATCH, M_HEADS, M_HEAD_DIM, M_HEAD_DIM), 0.1)
    inp['state_mlstm_n'] = nrm(ks[6], (DEPTH, DEC_BATCH, M_HEADS, M_HEAD_DIM), 0.5)
    inp['state_mlstm_m'] = jax.random.uniform(ks[7], (DEPTH, DEC_BATCH, M_HEADS), f32, 0.0, 2.0)
    inp['state_conv'] = nrm(ks[8], (DEPTH, DEC_BATCH, CONV_WIDTH - 1, QK_WIDTH), 1.0)
    inp['c_prompt'] = nrm(ks[9], (BATCH, D), 1.0)
    inp['c_sample'] = nrm(ks[10], (DEC_BATCH, D), 1.0)
    inp['w_ada'] = nrm(ks[11], (DEPTH, D, 6 * D), 0.5 * D ** -0.5)
    inp['b_ada'] = nrm(ks[12], (DEPTH, 6 * D), 0.02)
    inp['g_pre1'] = gain(ks[13], (DEPTH, D))
    inp['g_post1'] = gain(ks[14], (DEPTH, D))
    inp['g_pre2'] = gain(ks[15], (DEPTH, D))
    inp['g_post2'] = gain(ks[16], (DEPTH, D))
    inp['w_in'] = nrm(ks[17], (DEPTH, D, D_IN), D ** -0.5)
    inp['conv_w'] = nrm(ks[18], (DEPTH, CONV_WIDTH, QK_WIDTH), CONV_WIDTH ** -0.5)
    inp['conv_b'] = nrm(ks[19], (DEPTH, QK_WIDTH), 0.02)
    inp['b_igate'] = nrm(ks[20], (DEPTH, M_HEADS), 0.1)
    inp['b_fgate'] = jnp.linspace(3.0, 6.0, M_HEADS, dtype=f32)[None] + nrm(ks[21], (DEPTH, M_HEADS), 0.1)
    inp['mh_norm_g'] = gain(ks[22], (DEPTH, M_WIDTH))
    inp['w_a'] = nrm(ks[23], (DEPTH, M_WIDTH, D), M_WIDTH ** -0.5)
    inp['w_b'] = nrm(ks[24], (DEPTH, A_OUT_WIDTH, D), A_OUT_WIDTH ** -0.5)
    inp['w_out'] = nrm(ks[25], (DEPTH, D, D), D ** -0.5)
    inp['peer_wq'] = nrm(ks[26], (DEPTH, D, P_HEADS * P_QDIM), D ** -0.5)
    inp['peer_k1'] = nrm(ks[27], (DEPTH, P_NKEYS, P_HALF), P_HALF ** -0.5)
    inp['peer_k2'] = nrm(ks[28], (DEPTH, P_NKEYS, P_HALF), P_HALF ** -0.5)
    inp['peer_u'] = nrm(ks[29], (DEPTH, P_EXPERTS, D), D ** -0.5)
    inp['peer_v'] = nrm(ks[30], (DEPTH, P_EXPERTS, D), (P_HEADS * P_TOPK) ** -0.5)
    return inp

def reference(x_prompt, x_sample, cache_win0_kv, cache_win1_kv, cache_win2_kv,
              state_mlstm_C, state_mlstm_n, state_mlstm_m, state_conv,
              c_prompt, c_sample, w_ada, b_ada, g_pre1, g_post1, g_pre2, g_post2,
              w_in, conv_w, conv_b, b_igate, b_fgate, mh_norm_g, w_a, w_b, w_out,
              peer_wq, peer_k1, peer_k2, peer_u, peer_v):
    yp, ys = x_prompt, x_sample
    new_p, new_s = [], []
    for layer in range(DEPTH):
        prm = {
            'w_ada': w_ada[layer], 'b_ada': b_ada[layer],
            'g_pre1': g_pre1[layer], 'g_post1': g_post1[layer],
            'g_pre2': g_pre2[layer], 'g_post2': g_post2[layer],
            'w_in': w_in[layer], 'conv_w': conv_w[layer], 'conv_b': conv_b[layer],
            'b_igate': b_igate[layer], 'b_fgate': b_fgate[layer], 'mh_norm_g': mh_norm_g[layer],
            'w_a': w_a[layer], 'w_b': w_b[layer], 'w_out': w_out[layer],
            'peer_wq': peer_wq[layer], 'peer_k1': peer_k1[layer], 'peer_k2': peer_k2[layer],
            'peer_u': peer_u[layer], 'peer_v': peer_v[layer],
        }
        yp, sp = _layer(yp, c_prompt, None, prm)
        ys, ss = _layer(ys, c_sample, (cache_win0_kv[layer], cache_win1_kv[layer], cache_win2_kv[layer],
                                       state_mlstm_C[layer], state_mlstm_n[layer], state_mlstm_m[layer],
                                       state_conv[layer]), prm)
        new_p.append(sp)
        new_s.append(ss)
    win0_p, win1_p, win2_p, C_p, n_p, m_p, conv_p = (jnp.stack(z) for z in zip(*new_p))
    win0_s, win1_s, win2_s, C_s, n_s, m_s, conv_s = (jnp.stack(z) for z in zip(*new_s))
    return (yp, ys, win0_p, win1_p, win2_p, C_p, n_p, m_p, conv_p,
            win0_s, win1_s, win2_s, C_s, n_s, m_s, conv_s)


_drawn_inputs = setup_inputs


def setup_inputs(seed=0):
    import zlib

    import numpy as np

    out = dict(_drawn_inputs(seed))
    spreads = {}
    factors = {}
    for name, (base, spread) in spreads.items():
        noise = np.random.default_rng([zlib.crc32(name.encode()), seed]).standard_normal(out[name].shape)
        drawn = base * np.exp(spread * noise) if base else spread * noise
        out[name] = __import__('jax').numpy.asarray(drawn.astype(out[name].dtype))
    for name, factor in factors.items():
        out[name] = (out[name] * factor).astype(out[name].dtype)
    return out
```

```python
from contextlib import ExitStack

import numpy as np

import concourse.bass as bass
from concourse import mybir

F32 = mybir.dt.float32
U32 = mybir.dt.uint32
ALU = mybir.AluOpType
ACT = mybir.ActivationFunctionType
AX = mybir.AxisListType.X

P = 128
D = 1024
KD = D // P
SEQ = 512
PT = SEQ // P
NS, LS = 8, 8
TS = NS * LS
T = SEQ + TS
TH = T // 2
H = 4
G = 3
WINDOWS = (128, 512, 2048)
DILATIONS = (1, 4, 16)
RES = (1, 4, 8)
CW = 4
PH = 8
TOPK = 16
NKEYS = 128
SLOTS = PH * TOPK
EPS = 1e-6
SCALE = float(P) ** -0.5
NEG = -1e30
NC = NS + 1
CHUNK = 512
NR = 3
NCH = PT + 1


def tile_rows(i):
    return P if i < PT else TS


def heads_of(i):
    return PH if i < PT else PH // 2


def tile_cols(i):
    return slice(i * P, i * P + tile_rows(i))


def key_cols(i):
    own = (i + 1) * P
    band = min(i, 1) * P
    return [(0, own - P - band, P + band, 0), (1, 0, own, P + band), (2, 0, own, P + band + own)]


MASK_AT = np.cumsum([0] + [sum(n for _, _, n, _ in key_cols(i)) for i in range(PT)]).tolist()
NKMAX = MASK_AT[PT] - MASK_AT[PT - 1]


def constants():
    t = np.arange(P)[:, None]
    masks = np.zeros((P, MASK_AT[PT]), np.float32)
    for i in range(PT):
        for g, first, n, at in key_cols(i):
            dist = (i * P + t) - (first + np.arange(n)[None, :])
            ok = (dist >= 0) & (dist <= WINDOWS[g]) & (dist % DILATIONS[g] == 0)
            masks[:, MASK_AT[i] + at:MASK_AT[i] + at + n] = np.where(ok, 0.0, NEG)
    tok = np.arange(TS)
    seq, pos = tok // LS, tok % LS
    smask = np.zeros((TS, G, P + TS), np.float32)
    for g in range(G):
        r = pos % RES[g]
        kpos = DILATIONS[g] * np.arange(P)[None, :] + r[:, None]
        old = kpos >= pos[:, None]
        dist = pos[:, None] - pos[None, :]
        new = (seq[:, None] == seq[None, :]) & (dist >= 0) & (dist % DILATIONS[g] == 0)
        smask[:, g] = np.where(np.concatenate([old, new], 1), 0.0, NEG)
    s = np.arange(P)[:, None]
    tri = np.where(s <= np.arange(P)[None, :], 0.0, NEG)
    stri = np.full((P, TS), NEG)
    stri[:TS] = np.where((seq[:, None] == seq[None, :]) & (tok[:, None] <= tok[None, :]), 0.0, NEG)
    carry = np.ones(T)
    carry[0:SEQ:P] = 0.0
    carry[SEQ::LS] = 0.0
    restart = np.zeros(T)
    restart[SEQ::LS] = NEG
    sel = np.zeros((H, H, P))
    for h in range(H):
        sel[h, h] = 1.0
    f = lambda a: np.ascontiguousarray(a, dtype=np.float32)
    return {
        "c_ident": f(np.eye(P)), "c_masks": masks, "c_smask": f(smask.reshape(TS, -1)),
        "c_tri": f(tri), "c_stri": f(stri), "c_carry": f(np.tile(carry, (H, 1))),
        "c_restart": f(np.tile(restart, (H, 1))), "c_sel": f(sel.reshape(H, H * P)),
        "c_block": f((seq[:, None] == np.arange(NS)[None, :])),
        "c_fold": f(np.tile(np.eye(TS), (P // TS, 1))),
        "c_iota": f(np.tile(np.arange(TOPK), (P, 1))),
    }


def broadcast_mid(ap, n, at):
    dims = [list(x) for x in ap.ap]
    return bass.AP(ap.tensor, ap.offset, dims[:at] + [[0, n]] + dims[at:])


class Shared:
    pass


def roll_pieces(d):
    out = []
    for g in range(G):
        w, n = WINDOWS[g], max(1, WINDOWS[g] // 256)
        size = (w - LS) * D // n
        for s in range(NS):
            for c in range(n):
                at = c * size
                out.append((d[f"win{g}_s"][s, at:at + size].rearrange("(a n) -> a n", a=16),
                            d[f"cache{g}"][s, LS * D + at:LS * D + at + size].rearrange("(a n) -> a n", a=16)))
    return out


class Chain:

    def __init__(self, eng, sem):
        self.eng, self.sem, self.n = eng, sem, 0

    def step(self, ins):
        self.n += 1
        ins.then_inc(self.sem, 1)
        self.eng.wait_ge(self.sem, self.n)


def modulation(nc, k, d):
    NCK = 6 * D // CHUNK
    with ExitStack() as ctx:
        sb = lambda n, s, dt=F32: ctx.enter_context(nc.sbuf_tensor(n, s, dt))
        wring = sb("ada_ring", [P, NR, KD, CHUNK])
        cT = sb("ada_cT", [P, KD, NC])
        cs = sb("ada_cs", [P, KD, NC])
        mod = sb("ada_mod", [NC, 6, D])
        bias = sb("ada_bias", [NC, 6, D])
        grow = sb("ada_grow", [NC, 3, D])
        gcol = sb("ada_gcol", [P, KD])
        ready = [k.sem(f"ada_w_ready{r}") for r in range(NR)]
        s_c, s_b, s_silu, s_mm, s_add, s_tr, s_rows, s_chain, s_out, s_const = (
            k.sem("ada_" + n) for n in ("c", "bias", "silu", "mm", "add", "tr", "rows", "chain", "out", "const"))
        ps = k.ps
        with nc.Block() as block:
            @block.sync
            def _(sp):
                sp.dma_start(cT[:], d["cT"]).then_inc(s_c, 16)
                for n in range(NCK):
                    if n >= NR:
                        sp.wait_ge(s_mm, n - NR + 1)
                    sp.dma_start(wring[:, n % NR], d["w_ada"][n]).then_inc(ready[n % NR], 16)
                for j in range(4):
                    src, done = ((2, 1), (4, 2), (3, 2), (5, 3))[j]
                    sp.wait_ge(s_rows, done)
                    sp.dma_start(d["rows"][j], mod[:, src, :]).then_inc(s_out, 16)
                sp.wait_ge(s_out, 64)

            @block.scalar
            def _(act):
                for dst, src in ((k.ident, "c_ident"), (k.sel, "c_sel"), (k.block, "c_block"), (k.fold, "c_fold"),
                                 (k.iota, "c_iota"), (gcol, "g_pre1")):
                    act.dma_start(dst[:], d[src]).then_inc(s_const, 16)
                act.dma_start(bias[:].rearrange("p a n -> p (a n)"), d["b_ada"].partition_broadcast(NC)).then_inc(s_b, 16)
                for j, name in enumerate(("g_post1", "g_pre2", "g_post2")):
                    act.dma_start(grow[:, j], d[name].partition_broadcast(NC)).then_inc(s_b, 16)
                act.wait_ge(s_c, 16)
                act.activation(cs[:], cT[:], ACT.Silu).then_inc(s_silu, 1)

            @block.tensor
            def _(pe):
                pe.wait_ge(s_silu, 1)
                for n in range(NCK):
                    pe.wait_ge(ready[n % NR], 16 * (n // NR + 1))
                    if n >= 2:
                        pe.wait_ge(s_add, n - 1)
                    for c in range(KD):
                        mm = pe.matmul(ps[0:NC, n % 2, :], cs[:, c, :], wring[:, n % NR, c, :],
                                       start=c == 0, stop=c == KD - 1)
                    mm.then_inc(s_mm, 1)
                pe.wait_ge(s_add, NCK)
                pe.wait_ge(s_const, 96)
                for a in range(2):
                    for c in range(KD):
                        mm = pe.transpose(ps[:, 2 + a, c * NC:(c + 1) * NC], mod[:, a, c * P:(c + 1) * P],
                                          k.ident[0:NC, 0:NC])
                mm.then_inc(s_tr, 1)

            @block.vector
            def _(dve):
                chain = Chain(dve, s_chain)
                dve.wait_ge(s_b, 64)
                for n in range(NCK):
                    dve.wait_ge(s_mm, n + 1)
                    a, o = n // 2, (n % 2) * CHUNK
                    dve.tensor_tensor(mod[:, a, o:o + CHUNK], ps[0:NC, n % 2, :], bias[:, a, o:o + CHUNK],
                                      ALU.add).then_inc(s_add, 1)
                dve.wait_ge(s_add, NCK)
                dve.tensor_tensor(mod[:, 2], mod[:, 2], grow[:, 0], ALU.mult).then_inc(s_rows, 1)
                dve.scalar_tensor_tensor(mod[:, 4], mod[:, 4], 1.0, grow[:, 1], ALU.add, ALU.mult).then_inc(s_rows, 1)
                dve.tensor_tensor(mod[:, 5], mod[:, 5], grow[:, 2], ALU.mult).then_inc(s_rows, 1)
                dve.wait_ge(s_tr, 1)
                dve.wait_ge(s_const, 96)
                for c in range(KD):
                    dve.tensor_copy(k.shift1[:, c, :], ps[:, 2, c * NC:(c + 1) * NC])
                    ins = dve.tensor_scalar(k.scale1[:, c, :], ps[:, 3, c * NC:(c + 1) * NC], 1.0, gcol[:, c:c + 1],
                                            ALU.add, ALU.mult)
                chain.step(ins)


def normalised_input(nc, k, d):
    with ExitStack() as ctx:
        sb = lambda n, s, dt=F32: ctx.enter_context(nc.sbuf_tensor(n, s, dt))
        x = sb("ni_x", [P, NCH, D])
        junk = sb("ni_junk", [P, D])
        ss = sb("ni_ss", [P, NCH])
        ms = sb("ni_ms", [P, NCH])
        rt = sb("ni_rt", [P, NCH])
        s_x = [k.sem(f"ni_x{i}") for i in range(2)]
        s_sq, s_ms, s_rt, s_xn, s_tr, s_ev, s_chain = (
            k.sem("ni_" + n) for n in ("sq", "ms", "rt", "xn", "tr", "ev", "chain"))
        ps = k.ps
        with nc.Block() as block:
            @block.sync
            def _(sp):
                sp.dma_start(x[:, 0:PT, :], d["x_prompt"].rearrange("(t p) n -> p t n", p=P)).then_inc(s_x[0], 16)
                sp.dma_start(x[0:TS, PT, :], d["x_sample"]).then_inc(s_x[1], 16)

            @block.scalar
            def _(act):
                act.wait_ge(s_x[0], 16)
                act.wait_ge(s_x[1], 16)
                for i in range(NCH):
                    r = tile_rows(i)
                    ins = act.activation(junk[0:r], x[0:r, i, :], ACT.Square, accum_out=ss[0:r, i:i + 1])
                    ins.then_inc(s_sq, 1)
                    act.wait_ge(s_sq, i + 1)
                act.wait_ge(s_ms, 2)
                act.activation(rt[:, 0:PT], ms[:, 0:PT], ACT.Sqrt)
                act.activation(rt[0:TS, PT:NCH], ms[0:TS, PT:NCH], ACT.Sqrt).then_inc(s_rt, 1)
                for c in range(KD):
                    act.wait_ge(s_tr, c + 1)
                    act.activation(k.hT[:, c, 0:SEQ], ps[:, c % 4, :], ACT.Identity, scale=k.scale1[:, c, 0:1],
                                   bias=k.shift1[:, c, 0:1]).then_inc(s_ev, 1)

            @block.tensor
            def _(pe):
                pe.wait_ge(s_xn, NCH)
                for c in range(KD):
                    if c >= 4:
                        pe.wait_ge(s_ev, c - 3)
                    for i in range(PT):
                        pe.transpose(ps[:, c % 4, i * P:(i + 1) * P], x[:, i, c * P:(c + 1) * P], k.ident[:])
                    pe.transpose(ps[:, 4, c * TS:(c + 1) * TS], x[0:TS, PT, c * P:(c + 1) * P],
                                 k.ident[0:TS, 0:TS]).then_inc(s_tr, 1)

            @block.vector
            def _(dve):
                chain = Chain(dve, s_chain)
                dve.wait_ge(s_sq, NCH)
                dve.tensor_scalar(ms[:, 0:PT], ss[:, 0:PT], 1.0 / D, EPS, ALU.mult, ALU.add).then_inc(s_ms, 1)
                dve.tensor_scalar(ms[0:TS, PT:NCH], ss[0:TS, PT:NCH], 1.0 / D, EPS, ALU.mult, ALU.add).then_inc(s_ms, 1)
                dve.wait_ge(s_rt, 1)
                dve.reciprocal(ss[:, 0:PT], rt[:, 0:PT])
                chain.step(dve.reciprocal(ss[0:TS, PT:NCH], rt[0:TS, PT:NCH]))
                for i in range(NCH):
                    r = tile_rows(i)
                    dve.tensor_scalar(x[0:r, i, :], x[0:r, i, :], ss[0:r, i:i + 1], None, ALU.mult).then_inc(s_xn, 1)
                dve.wait_ge(s_tr, KD)
                for c in range(KD):
                    out = k.hT[:, c, SEQ:T].rearrange("p (s l) -> p s l", s=NS)
                    src = ps[:, 4, c * TS:(c + 1) * TS].rearrange("p (s l) -> p s l", s=NS)
                    ins = dve.tensor_tensor(out, src, broadcast_mid(k.scale1[:, c, 1:NC], LS, 2), ALU.mult)
                chain.step(ins)
                for c in range(KD):
                    out = k.hT[:, c, SEQ:T].rearrange("p (s l) -> p s l", s=NS)
                    ins = dve.tensor_tensor(out, out, broadcast_mid(k.shift1[:, c, 1:NC], LS, 2), ALU.add)
                chain.step(ins)


def project(nc, k, name, rhsT, jobs):
    units = []
    for n, (kind, _, _) in enumerate(jobs):
        units += [(n, j) for j in range(CHUNK // P if kind == "feature" else NCH)]
    last_unit = {}
    for u, (n, _) in enumerate(units):
        last_unit[n] = u
    with ExitStack() as ctx:
        wring = ctx.enter_context(nc.sbuf_tensor(name + "_ring", [P, NR, KD, CHUNK], F32))
        ready = [k.sem(f"{name}_w_ready{r}") for r in range(NR)]
        s_mm, s_ev = k.sem(name + "_mm"), k.sem(name + "_taken")
        ps = k.ps
        with nc.Block() as block:
            @block.gpsimd
            def _(pool):
                for u in range(len(units)):
                    if k.rolls:
                        pool.wait_ge(s_mm, u + 1)
                        dst, src = k.rolls.pop()
                        pool.dma_start(dst, src).then_inc(k.s_roll, 16)

            @block.sync
            def _(sp):
                for n, (_, src, _) in enumerate(jobs):
                    if n >= NR:
                        sp.wait_ge(s_mm, last_unit[n - NR] + 1)
                    sp.dma_start(wring[:, n % NR], src).then_inc(ready[n % NR], 16)

            @block.tensor
            def _(pe):
                for u, (n, j) in enumerate(units):
                    if j == 0:
                        pe.wait_ge(ready[n % NR], 16 * (n // NR + 1))
                    if u >= 2:
                        pe.wait_ge(s_ev, u - 1)
                    w = wring[:, n % NR]
                    for c in range(KD):
                        on = dict(start=c == 0, stop=c == KD - 1)
                        if jobs[n][0] == "feature":
                            wc = w[:, c, j * P:(j + 1) * P]
                            pe.matmul(ps[:, u % 2, 0:TH], wc, rhsT[:, c, 0:TH], **on)
                            mm = pe.matmul(ps[:, 2 + u % 2, 0:TH], wc, rhsT[:, c, TH:T], **on)
                        else:
                            r = tile_rows(j)
                            mm = pe.matmul(ps[0:r, u % 2, :], rhsT[:, c, tile_cols(j)], w[:, c, :], **on)
                    mm.then_inc(s_mm, 1)

            @block.scalar
            def _(act):
                for u, (n, j) in enumerate(units):
                    act.wait_ge(s_mm, u + 1)
                    if jobs[n][0] == "feature":
                        ins = jobs[n][2](act, j, (ps[:, u % 2, 0:TH], ps[:, 2 + u % 2, 0:TH]))
                    else:
                        r = tile_rows(j)
                        ins = jobs[n][2](act, j, r, ps[0:r, u % 2, :])
                    ins.then_inc(s_ev, 1)


def attention_projections(nc, k, d, a):
    jobs = []
    for n in range(2 * G):
        def take(act, j, halves, n=n):
            act.activation(a.qk[:, H * n + j, 0:TH], halves[0], ACT.Copy)
            act.activation(a.qk[:, H * n + j, TH:SEQ], halves[1][:, 0:SEQ - TH], ACT.Copy)
            return act.activation(k.qkS[:, H * n + j, :], halves[1][:, SEQ - TH:], ACT.Copy)
        jobs.append(("feature", d["w_attn_qk"][n], take))
    for g in range(G):
        def take(act, j, r, res, g=g):
            return act.activation(a.v[:, j, g, :] if j < PT else k.vS[:, g, :], res, ACT.Copy)
        jobs.append(("token", d["w_attn_v"][g], take))
    project(nc, k, "ap", k.hT, jobs)


def prompt_attention(nc, k, d, a):
    steps = [(i, h) for i in range(PT) for h in range(H)]
    N = len(steps)
    with ExitStack() as ctx:
        sb = lambda n, s, dt=F32: ctx.enter_context(nc.sbuf_tensor(n, s, dt))
        masks = sb("pa_masks", [P, MASK_AT[PT]])
        prob = sb("pa_prob", [P, 2, NKMAX])
        probT = sb("pa_probT", [P, 2, NKMAX])
        mx = sb("pa_mx", [P, N, 4])
        nb = sb("pa_nb", [P, N])
        den = sb("pa_den", [P, N])
        rden = sb("pa_rden", [P, N])
        s_m, s_s, s_max, s_exp, s_norm, s_t, s_te, s_pv, s_o, s_chain, s_kv = (
            k.sem("pa_" + n) for n in ("masks", "scores", "max", "exp", "norm", "turned", "turned_taken", "pv",
                                       "out", "chain", "kv"))
        ps = k.ps
        flat = ps[:, 3:6, :].rearrange("p b n -> p (b n)")
        with nc.Block() as block:
            @block.sync
            def _(sp):
                sp.dma_start(masks[:], d["c_masks"]).then_inc(s_m, 16)
                for g in range(G):
                    sp.dma_start(d["kT_p"][g], a.qk[:, (2 * g + 1) * H:(2 * g + 2) * H, :]).then_inc(s_kv, 16)
                    sp.dma_start(d["v_p"][g], a.v[:, :, g, :]).then_inc(s_kv, 16)
                sp.wait_ge(s_kv, 16 * 2 * G)

            @block.tensor
            def _(pe):
                def scores(s):
                    i, h = steps[s]
                    if s >= 1:
                        pe.wait_ge(s_max, s)
                    for g, first, n, _ in key_cols(i):
                        mm = pe.matmul(ps[:, g, 0:n], a.qk[:, 2 * g * H + h, i * P:(i + 1) * P],
                                       a.qk[:, (2 * g + 1) * H + h, first:first + n], start=True, stop=True)
                    mm.then_inc(s_s, 1)

                scores(0)
                for s, (i, h) in enumerate(steps):
                    if s + 1 < N:
                        scores(s + 1)
                    pe.wait_ge(s_norm, s + 1)
                    if s >= 1:
                        pe.wait_ge(s_te, s)
                    nk = sum(n for _, _, n, _ in key_cols(i)) // P
                    for b in range(nk):
                        mm = pe.transpose(flat[:, b * P:(b + 1) * P], prob[:, s % 2, b * P:(b + 1) * P], k.ident[:])
                    mm.then_inc(s_t, 1)
                    pe.wait_ge(s_te, s + 1)
                    if s >= 2:
                        pe.wait_ge(s_o, s - 1)
                    b = 0
                    for g, first, n, _ in key_cols(i):
                        for t in range(first // P, (first + n) // P):
                            mm = pe.matmul(ps[:, 6 + s % 2, 0:P], a.v[:, t, g, h * P:(h + 1) * P],
                                           probT[:, s % 2, b * P:(b + 1) * P], start=b == 0, stop=b == nk - 1)
                            b += 1
                    mm.then_inc(s_pv, 1)

            @block.vector
            def _(dve):
                chain = Chain(dve, s_chain)
                dve.wait_ge(s_m, 16)
                for s, (i, h) in enumerate(steps):
                    dve.wait_ge(s_s, s + 1)
                    if s >= 2:
                        dve.wait_ge(s_t, s - 1)
                    for g, first, n, at in key_cols(i):
                        ins = dve.tensor_tensor_reduce(prob[:, s % 2, at:at + n], ps[:, g, 0:n],
                                                       masks[:, MASK_AT[i] + at:MASK_AT[i] + at + n], 1.0, 2 * NEG,
                                                       ALU.add, ALU.max, mx[:, s, g:g + 1])
                    chain.step(ins)
                    chain.step(dve.tensor_reduce(mx[:, s, 3:4], mx[:, s, 0:G], AX, ALU.max))
                    dve.tensor_scalar(nb[:, s:s + 1], mx[:, s, 3:4], -SCALE, None, ALU.mult).then_inc(s_max, 1)
                    dve.wait_ge(s_exp, s + 1)
                    chain.step(dve.reciprocal(rden[:, s:s + 1], den[:, s:s + 1]))
                    nk = sum(n for _, _, n, _ in key_cols(i))
                    dve.tensor_scalar(prob[:, s % 2, 0:nk], prob[:, s % 2, 0:nk], rden[:, s:s + 1], None,
                                      ALU.mult).then_inc(s_norm, 1)

            @block.scalar
            def _(act):
                def turned(s):
                    i, h = steps[s]
                    nk = sum(n for _, _, n, _ in key_cols(i))
                    act.wait_ge(s_t, s + 1)
                    if s >= 2:
                        act.wait_ge(s_pv, s - 1)
                    for b in range(0, nk, 512):
                        m = min(512, nk - b)
                        ins = act.activation(probT[:, s % 2, b:b + m], flat[:, b:b + m], ACT.Copy)
                    ins.then_inc(s_te, 1)
                    act.wait_ge(s_pv, s + 1)
                    act.activation(k.oaT[:, h, i * P:(i + 1) * P], ps[:, 6 + s % 2, 0:P], ACT.Copy).then_inc(s_o, 1)

                for s, (i, h) in enumerate(steps):
                    nk = sum(n for _, _, n, _ in key_cols(i))
                    act.wait_ge(s_max, s + 1)
                    act.activation(prob[:, s % 2, 0:nk], prob[:, s % 2, 0:nk], ACT.Exp, bias=nb[:, s:s + 1],
                                   scale=SCALE, accum_out=den[:, s:s + 1]).then_inc(s_exp, 1)
                    if s >= 1:
                        turned(s - 1)
                turned(N - 1)


def mlstm_projections(nc, k, d, m):
    def take_raw(n):
        def take(act, j, halves):
            b = H * n + j
            act.activation(m.raw[:, b, CW - 1:CW - 1 + TH], halves[0], ACT.Copy)
            act.activation(m.raw[:, b, CW - 1 + TH:CW - 1 + SEQ], halves[1][:, 0:SEQ - TH], ACT.Copy)
            sample = halves[1][:, SEQ - TH:]
            out = m.rawS[:, b].rearrange("p (s l) -> p s l", s=NS)[:, :, CW - 1:CW - 1 + LS]
            return act.activation(out, sample.rearrange("p (s l) -> p s l", s=NS), ACT.Copy)
        return take

    def take_v(act, j, r, res):
        return act.activation(m.v[0:r, j, :], res, ACT.Copy)

    def take_o(act, j, r, res):
        return act.activation(m.o[0:r, j, :], res, ACT.Sigmoid)

    project(nc, k, "mp", k.hT, [("feature", d["w_qk"][0], take_raw(0)), ("feature", d["w_qk"][1], take_raw(1)),
                                ("token", d["w_mv"], take_v), ("token", d["w_mo"], take_o)])


A_, W_, E_, X_ = range(4)


def conv_and_gates(nc, k, d, m):
    RAWS = NS * (CW - 1 + LS)
    with ExitStack() as ctx:
        sb = lambda n, s, dt=F32: ctx.enter_context(nc.sbuf_tensor(n, s, dt))
        state = sb("cg_state", [P, 2 * H, NS, CW - 1])
        cw = sb("cg_w", [P, 2 * H, CW + 1])
        acc = sb("cg_acc", [P, 2 * H, T])
        newp = sb("cg_newp", [P, 2 * H, CW - 1])
        news = sb("cg_news", [P, 2 * H, NS, CW - 1])
        wg = sb("cg_wg", [P, KD, 2 * H])
        gb = sb("cg_gb", [H, 2])
        m0 = sb("cg_m0", [H, NS])
        carry = sb("cg_carry", [H, T])
        restart = sb("cg_restart", [H, T])
        ig = sb("cg_ig", [H, T])
        fg = sb("cg_fg", [H, T])
        lf = sb("cg_lf", [H, T])
        e = sb("cg_e", [H, T])
        bb = sb("cg_b", [H, T])
        mt = sb("cg_mt", [H, T])
        mprev = sb("cg_mprev", [H, PT + NS])
        mlast = sb("cg_mlast", [H, PT + NS])
        mnew = sb("cg_mnew", [H, 1 + NS])
        s_in, s_st, s_gm, s_gt, s_lf, s_f, s_cv, s_silu, s_rows, s_exp, s_tr, s_chain, s_out, s_new, s_mn, s_sc = (
            k.sem("cg_" + n) for n in ("in", "state", "gate_mm", "gate_taken", "logf", "f_abs", "conv", "silu", "rows",
                                       "exp", "turned", "chain", "out", "new", "mnew", "kscale"))
        s_one = k.sem("cg_act")
        ps = k.ps

        def rows(t):
            return t[:, 0:SEQ].rearrange("h (c t) -> h c t", c=PT), t[:, SEQ:T].rearrange("h (s l) -> h s l", s=NS)

        with nc.Block() as block:
            @block.sync
            def _(sp):
                for dst, src in ((state[:], "stateT"), (cw[:], "conv_w"), (wg[:], "w_gates"), (gb[:], "b_gates"),
                                 (m0[:], "m0"), (carry[:], "c_carry"), (restart[:], "c_restart")):
                    sp.dma_start(dst, d[src]).then_inc(s_in, 16)
                sp.wait_ge(s_new, 2)
                sp.dma_start(d["conv_p"], newp[:]).then_inc(s_out, 16)
                sp.dma_start(d["conv_s"], news[:]).then_inc(s_out, 16)
                sp.wait_ge(s_mn, 2)
                sp.dma_start(d["m_new"], mnew[:]).then_inc(s_out, 16)
                sp.wait_ge(s_out, 48)

            @block.gpsimd
            def _(pool):
                pool.memset(m.ones[:], 1.0)
                pool.wait_ge(s_silu, 2 * H)
                for b in range(H, 2 * H):
                    ins = pool.tensor_scalar(m.qk[:, b, :], m.qk[:, b, :], SCALE, None, ALU.mult)
                ins.then_inc(s_sc, 1)
                pool.wait_ge(s_sc, 1)

            @block.tensor
            def _(pe):
                pe.wait_ge(s_in, 7 * 16)
                for gate in range(2):
                    for part, cols in ((0, slice(0, SEQ)), (1, slice(SEQ, T))):
                        n = cols.stop - cols.start
                        for c in range(KD):
                            mm = pe.matmul(ps[0:H, 2 * gate + part, 0:n], wg[:, c, gate * H:(gate + 1) * H],
                                           k.hT[:, c, cols], start=c == 0, stop=c == KD - 1)
                mm.then_inc(s_gm, 1)
                pe.wait_ge(s_exp, 1)
                for c in range(NCH):
                    r = tile_rows(c)
                    for kind in range(4):
                        o = (c * 4 + kind) * H
                        mm = pe.matmul(ps[0:r, 4, o:o + H], m.rows[:, kind, tile_cols(c)], k.ident[0:H, 0:H],
                                       start=True, stop=True)
                for h in range(H):
                    mm = pe.matmul(ps[:, 5, h * (PT + NS):(h + 1) * (PT + NS)], k.sel[:, h * P:(h + 1) * P],
                                   m.decay[:], start=True, stop=True)
                mm.then_inc(s_tr, 1)

            @block.scalar
            def _(act):
                chain = Chain(act, s_one)
                act.wait_ge(s_gm, 1)
                for gate, dst in ((0, ig), (1, fg)):
                    act.activation(dst[:, 0:SEQ], ps[0:H, 2 * gate, :], ACT.Identity, bias=gb[:, gate:gate + 1])
                    ins = act.activation(dst[:, SEQ:T], ps[0:H, 2 * gate + 1, 0:TS], ACT.Identity,
                                         bias=gb[:, gate:gate + 1])
                chain.step(ins)
                chain.step(act.activation(e[:], fg[:], ACT.Abs))
                chain.step(act.activation(e[:], e[:], ACT.Exp, scale=-1.0))
                act.activation(e[:], e[:], ACT.Ln, bias=1.0).then_inc(s_f, 1)
                act.wait_ge(s_rows, 1)
                for kind in (A_, W_, E_, X_):
                    if kind != A_:
                        ins = act.activation(m.rows[:, kind, :], m.rows[:, kind, :], ACT.Exp)
                act.activation(m.decay[:], m.decay[:], ACT.Exp).then_inc(s_exp, 1)
                for b in range(2 * H):
                    act.wait_ge(s_cv, b + 1)
                    act.activation(m.qk[:, b, :], acc[:, b, :], ACT.Silu).then_inc(s_silu, 1)

            @block.vector
            def _(dve):
                chain = Chain(dve, s_chain)
                dve.wait_ge(s_in, 7 * 16)
                dve.memset(m.raw[:, :, 0:CW - 1], 0.0)
                head = m.rawS[:].rearrange("p b (s l) -> p b s l", s=NS)
                for b in range(2 * H):
                    ins = dve.tensor_copy(head[:, b, :, 0:CW - 1], state[:, b])
                chain.step(ins)
                dve.tensor_copy(newp[:], m.raw[:, :, SEQ:SEQ + CW - 1]).then_inc(s_new, 1)
                for b in range(2 * H):
                    ins = dve.tensor_copy(news[:, b], head[:, b, :, LS:LS + CW - 1])
                ins.then_inc(s_new, 1)
                dve.wait_ge(s_f, 1)
                dve.memset(mprev[:, 0:1], 0.0)
                chain.step(dve.tensor_scalar(lf[:], fg[:], 0.0, None, ALU.min))
                chain.step(dve.tensor_tensor(lf[:], lf[:], e[:], ALU.subtract))
                chain.step(dve.tensor_tensor_scan(bb[:], carry[:], lf[:], 0.0, ALU.mult, ALU.add))
                first = lambda t: t[:, SEQ:T].rearrange("h (s l) -> h s l", s=NS)[:, :, 0]
                dve.tensor_copy(e[:], ig[:])
                chain.step(dve.tensor_tensor(mprev[:, PT:], first(lf), m0[:], ALU.add))
                chain.step(dve.tensor_tensor(first(e), first(e), mprev[:, PT:], ALU.max))
                chain.step(dve.tensor_tensor(fg[:], lf[:], restart[:], ALU.add))
                chain.step(dve.tensor_tensor_scan(mt[:], fg[:], e[:], 0.0, ALU.add, ALU.max))
                mtp, mts = rows(mt)
                bp, bs = rows(bb)
                dve.tensor_copy(mprev[:, 1:PT], mtp[:, 0:PT - 1, P - 1])
                dve.tensor_copy(mprev[:, PT:], m0[:])
                dve.tensor_copy(mnew[:, 0:1], mtp[:, PT - 1, P - 1:P])
                dve.tensor_copy(mnew[:, 1:], mts[:, :, LS - 1]).then_inc(s_mn, 2)
                chain.step(dve.tensor_tensor(m.M[:], mt[:], bb[:], ALU.subtract))
                Mp, Ms = rows(m.M)
                dve.tensor_copy(mlast[:, 0:PT], Mp[:, :, P - 1])
                dve.tensor_copy(mlast[:, PT:], Ms[:, :, LS - 1])
                chain.step(dve.tensor_tensor(m.rows[:, A_, :], ig[:], bb[:], ALU.subtract))
                chain.step(dve.tensor_scalar(m.rows[:, E_, :], mt[:], -1.0, None, ALU.mult))
                for kind, sign in ((W_, 0), (X_, 1)):
                    outp, outs = rows(m.rows[:, kind, :])
                    if kind == W_:
                        dve.tensor_tensor(outp, broadcast_mid(mprev[:, 0:PT], P, 2), Mp, ALU.subtract)
                        dve.tensor_tensor(outs, broadcast_mid(mprev[:, PT:], LS, 2), Ms, ALU.subtract)
                    else:
                        ap_, as_ = rows(m.rows[:, A_, :])
                        dve.tensor_tensor(outp, ap_, broadcast_mid(mlast[:, 0:PT], P, 2), ALU.subtract)
                        dve.tensor_tensor(outs, as_, broadcast_mid(mlast[:, PT:], LS, 2), ALU.subtract)
                dve.tensor_tensor(m.decay[:], mprev[:], mlast[:], ALU.subtract).then_inc(s_rows, 1)
                for b in range(2 * H):
                    raw = m.raw[:, b, :]
                    rs = m.rawS[:, b].rearrange("p (s l) -> p s l", s=NS)
                    op, os_ = acc[:, b, 0:SEQ], acc[:, b, SEQ:T].rearrange("p (s l) -> p s l", s=NS)
                    dve.tensor_scalar(op, raw[:, 0:SEQ], cw[:, b, 0:1], cw[:, b, CW:CW + 1], ALU.mult, ALU.add)
                    chain.step(dve.tensor_scalar(os_, rs[:, :, 0:LS], cw[:, b, 0:1], cw[:, b, CW:CW + 1],
                                                 ALU.mult, ALU.add))
                    for j in range(1, CW):
                        dve.scalar_tensor_tensor(op, raw[:, j:j + SEQ], cw[:, b, j:j + 1], op, ALU.mult, ALU.add)
                        ins = dve.scalar_tensor_tensor(os_, rs[:, :, j:j + LS], cw[:, b, j:j + 1], os_,
                                                       ALU.mult, ALU.add)
                        if j < CW - 1:
                            chain.step(ins)
                    ins.then_inc(s_cv, 1)
                dve.wait_ge(s_tr, 1)
                for c in range(NCH):
                    r = tile_rows(c)
                    dve.tensor_copy(m.cols[0:r, c], ps[0:r, 4, c * 16:(c + 1) * 16].rearrange("p (k h) -> p k h", k=4))
                chain.step(dve.tensor_copy(m.dcols[:], ps[:, 5, 0:H * (PT + NS)].rearrange("p (h n) -> p h n", h=H)))


def mlstm(nc, k, d, m):
    LAST = NCH - 1
    with ExitStack() as ctx:
        sb = lambda n, s, dt=F32: ctx.enter_context(nc.sbuf_tensor(n, s, dt))
        C = sb("ml_C", [P, H, P])
        n_ = sb("ml_n", [P, H])
        C0 = sb("ml_C0", [P, NS, H, P])
        n0 = sb("ml_n0", [P, NS, H])
        tri = sb("ml_tri", [P, P])
        stri = sb("ml_stri", [P, TS])
        mhg = sb("ml_mhg", [P, H])
        w = sb("ml_w", [P, H, P])
        sT = sb("ml_sT", [P, H, P])
        kw = sb("ml_kw", [P, H, P])
        ks = sb("ml_ks", [P, 2, H, P])
        iw = sb("ml_iw", [P, H, P])
        hn = sb("ml_hn", [P, H, P])
        sq = sb("ml_sq", [P, H, P])
        dn = sb("ml_dn", [P, H])
        rd = sb("ml_rd", [P, H])
        ss = sb("ml_ss", [P, H])
        ms = sb("ml_ms", [P, H])
        rt = sb("ml_rt", [P, H])
        qm = sb("ml_qm", [P, H, NS * (TS + LS)])
        s_in, s_pre, s_e, s_w, s_s, s_mid, s_iw, s_ms, s_rt, s_hn, s_tr, s_tt, s_c, s_ks, s_su, s_sc, s_z, s_qm, s_out, s_chain = (
            k.sem("ml_" + n) for n in ("in", "pre", "expo", "w", "s", "mid", "inter", "ms", "root", "h", "turned",
                                       "turned_taken", "state", "kmask", "seq_update", "seq_state", "zero", "qmask",
                                       "out", "chain"))
        ps = k.ps
        by_head = lambda bank, r: ps[0:r, bank, :].rearrange("p (h t) -> p h t", h=H)
        with nc.Block() as block:
            @block.sync
            def _(sp):
                sp.dma_start(tri[:], d["c_tri"]).then_inc(s_in, 16)
                sp.dma_start(stri[:], d["c_stri"]).then_inc(s_in, 16)
                sp.dma_start(mhg[:], d["mh_norm_g"]).then_inc(s_in, 16)
                sp.dma_start(C0[:], d["C0"]).then_inc(s_in, 16)
                sp.dma_start(n0[:], d["n0"]).then_inc(s_in, 16)
                sp.wait_ge(s_c, PT)
                sp.dma_start(d["C_p"], C[:]).then_inc(s_out, 16)
                sp.dma_start(d["n_p"], n_[:]).then_inc(s_out, 16)
                sp.wait_ge(s_sc, NS)
                sp.dma_start(d["C_s"], C0[:]).then_inc(s_out, 16)
                sp.dma_start(d["n_s"], n0[:]).then_inc(s_out, 16)
                sp.wait_ge(s_out, 64)

            @block.gpsimd
            def _(pool):
                pool.memset(C[:], 0.0).then_inc(s_z, 1)
                pool.memset(n_[:], 0.0).then_inc(s_z, 1)
                pool.memset(qm[:], 0.0).then_inc(s_z, 1)
                pool.wait_ge(s_z, 3)
                for h in range(H):
                    out = qm[:, h, :].rearrange("p (s r) -> p s r", r=TS + LS)[:, :, 0:LS]
                    ins = pool.tensor_copy(out, m.qk[:, h, SEQ:T].rearrange("p (s l) -> p s l", s=NS))
                ins.then_inc(s_qm, 1)

            @block.tensor
            def _(pe):
                for c in range(NCH):
                    r, cols = tile_rows(c), tile_cols(c)
                    if c >= 1:
                        pe.wait_ge(s_c, c)
                        pe.wait_ge(s_iw, c)
                        pe.wait_ge(s_hn, c)
                    for h in range(H):
                        o = h * P
                        pe.transpose(ps[0:r, 0, o:o + P], m.qk[:, H + h, cols], k.ident[:])
                        pe.matmul(ps[0:r, 1, o:o + r], k.sel[:, o:o + r], m.M[:, cols], start=True, stop=True)
                        mm = pe.matmul(ps[0:r, 2, o:o + r], m.qk[:, H + h, cols], m.qk[:, h, cols],
                                       start=True, stop=True)
                    mm.then_inc(s_pre, 1)
                    pe.wait_ge(s_s, c + 1)
                    if c == 0:
                        pe.wait_ge(s_z, 3)
                    if c == LAST:
                        pe.wait_ge(s_qm, 1)
                        pe.wait_ge(s_in, 80)
                    for h in range(H):
                        o = h * P
                        vh = m.v[0:r, c, o:o + P]
                        pe.matmul(ps[0:r, 1, o:o + P], sT[0:r, h, 0:r], vh, start=True, stop=True)
                        pe.matmul(ps[0:r, 0, h:h + 1], sT[0:r, h, 0:r], m.ones[0:r, 0:1], start=True, stop=True)
                        if c < LAST:
                            pe.matmul(ps[0:r, 2, o:o + P], m.qk[:, h, cols], C[:, h, :], start=True, stop=True)
                            pe.matmul(ps[0:r, 0, H + h:H + h + 1], m.qk[:, h, cols], n_[:, h:h + 1],
                                      start=True, stop=True)
                            pe.matmul(ps[:, 3, o:o + P], kw[0:r, h, :], vh, start=True, stop=True)
                            mm = pe.matmul(ps[:, 0, 2 * H + h:2 * H + h + 1], kw[0:r, h, :], m.ones[0:r, 0:1],
                                           start=True, stop=True)
                        else:
                            for s in range(NS):
                                on = dict(start=s == 0, stop=s == NS - 1)
                                q = qm[:, h, s * TS:(s + 1) * TS]
                                pe.matmul(ps[0:r, 2, o:o + P], q, C0[:, s, h, :], **on)
                            for s in range(NS):
                                on = dict(start=s == 0, stop=s == NS - 1)
                                q = qm[:, h, s * TS:(s + 1) * TS]
                                mm = pe.matmul(ps[0:r, 0, H + h:H + h + 1], q, n0[:, s, h:h + 1], **on)
                    mm.then_inc(s_mid, 1)
                    pe.wait_ge(s_hn, c + 1)
                    if c >= 1:
                        pe.wait_ge(s_tt, c)
                    for h in range(H):
                        mm = pe.transpose(ps[:, 4, h * P:h * P + r], hn[0:r, h, :], k.ident[0:r, 0:r])
                    mm.then_inc(s_tr, 1)
                for s in range(NS):
                    pe.wait_ge(s_ks, s + 1)
                    if s >= 2:
                        pe.wait_ge(s_sc, s - 1)
                    for h in range(H):
                        pe.matmul(ps[:, 5 + s % 2, h * P:(h + 1) * P], ks[0:TS, s % 2, h, :],
                                  m.v[0:TS, LAST, h * P:(h + 1) * P], start=True, stop=True)
                        mm = pe.matmul(ps[:, 3 if s % 2 else 7, h:h + 1], ks[0:TS, s % 2, h, :], m.ones[0:TS, 0:1],
                                       start=True, stop=True)
                    mm.then_inc(s_su, 1)

            @block.scalar
            def _(act):
                for c in range(NCH):
                    r, cols = tile_rows(c), tile_cols(c)
                    act.wait_ge(s_e, c + 1)
                    for h in range(H):
                        ins = act.activation(w[0:r, h, 0:r], w[0:r, h, 0:r], ACT.Exp, bias=m.cols[0:r, c, A_, h:h + 1])
                    ins.then_inc(s_w, 1)
                    act.wait_ge(s_mid, c + 1)
                    for h in range(H):
                        ins = act.activation(iw[0:r, h, :], by_head(2, r)[:, h, :], ACT.Copy,
                                             scale=m.cols[0:r, c, W_, h:h + 1])
                    ins.then_inc(s_iw, 1)
                    act.wait_ge(s_ms, c + 1)
                    act.activation(rt[0:r], ms[0:r], ACT.Sqrt).then_inc(s_rt, 1)
                    act.wait_ge(s_tr, c + 1)
                    act.wait_ge(s_in, 80)
                    for h in range(H):
                        ins = act.activation(k.hmT[:, h, cols], ps[:, 4, h * P:h * P + r], ACT.Copy,
                                             scale=mhg[:, h:h + 1])
                    ins.then_inc(s_tt, 1)

            @block.vector
            def _(dve):
                chain = Chain(dve, s_chain)
                dve.wait_ge(s_in, 80)
                for c in range(NCH):
                    r = tile_rows(c)
                    mask = tri[0:r, 0:r] if c < LAST else stri[0:r, 0:r]
                    dve.wait_ge(s_pre, c + 1)
                    dve.tensor_tensor(w[0:r, :, 0:r], broadcast_mid(mask, H, 1), by_head(1, r)[:, :, 0:r],
                                      ALU.subtract).then_inc(s_e, 1)
                    for h in range(H):
                        dve.tensor_scalar(kw[0:r, h, :], by_head(0, r)[:, h, :], m.cols[0:r, c, X_, h:h + 1], None,
                                          ALU.mult)
                    dve.wait_ge(s_w, c + 1)
                    dve.tensor_tensor(sT[0:r, :, 0:r], w[0:r, :, 0:r], by_head(2, r)[:, :, 0:r],
                                      ALU.mult).then_inc(s_s, 1)
                    dve.wait_ge(s_mid, c + 1)
                    chain.step(dve.tensor_tensor(dn[0:r], ps[0:r, 0, H:2 * H], m.cols[0:r, c, W_, :], ALU.mult))
                    chain.step(dve.tensor_tensor(dn[0:r], ps[0:r, 0, 0:H], dn[0:r], ALU.add))
                    chain.step(dve.scalar_tensor_tensor(dn[0:r], dn[0:r], -1.0, dn[0:r], ALU.mult, ALU.max))
                    chain.step(dve.tensor_tensor(dn[0:r], dn[0:r], m.cols[0:r, c, E_, :], ALU.max))
                    chain.step(dve.reciprocal(rd[0:r], dn[0:r]))
                    if c < LAST:
                        for h in range(H):
                            dc = m.dcols[:, h, c:c + 1]
                            dve.scalar_tensor_tensor(C[:, h, :], C[:, h, :], dc, ps[:, 3, h * P:(h + 1) * P],
                                                     ALU.mult, ALU.add)
                            ins = dve.scalar_tensor_tensor(n_[:, h:h + 1], n_[:, h:h + 1], dc,
                                                           ps[:, 0, 2 * H + h:2 * H + h + 1], ALU.mult, ALU.add)
                        ins.then_inc(s_c, 1)
                    dve.wait_ge(s_iw, c + 1)
                    chain.step(dve.tensor_tensor(hn[0:r], iw[0:r], by_head(1, r), ALU.add))
                    chain.step(dve.tensor_tensor(hn[0:r], hn[0:r],
                                                 m.o[0:r, c, :].rearrange("p (h t) -> p h t", h=H), ALU.mult))
                    chain.step(dve.tensor_tensor(hn[0:r], hn[0:r], broadcast_mid(rd[0:r], P, 2), ALU.mult))
                    chain.step(dve.tensor_tensor(sq[0:r], hn[0:r], hn[0:r], ALU.mult))
                    chain.step(dve.tensor_reduce(ss[0:r], sq[0:r], AX, ALU.add))
                    dve.tensor_scalar(ms[0:r], ss[0:r], 1.0 / P, EPS, ALU.mult, ALU.add).then_inc(s_ms, 1)
                    dve.wait_ge(s_rt, c + 1)
                    chain.step(dve.reciprocal(rd[0:r], rt[0:r]))
                    dve.tensor_tensor(hn[0:r], hn[0:r], broadcast_mid(rd[0:r], P, 2), ALU.mult).then_inc(s_hn, 1)
                    dve.wait_ge(s_tr, c + 1)
                for s in range(NS + 1):
                    if s < NS:
                        if s >= 2:
                            dve.wait_ge(s_su, s - 1)
                        dve.tensor_scalar(ks[0:TS, s % 2], kw[0:TS], k.block[:, s:s + 1], None,
                                          ALU.mult).then_inc(s_ks, 1)
                    if s >= 1:
                        q = s - 1
                        dve.wait_ge(s_su, q + 1)
                        for h in range(H):
                            dc = m.dcols[:, h, PT + q:PT + q + 1]
                            dve.scalar_tensor_tensor(C0[:, q, h, :], C0[:, q, h, :], dc,
                                                     ps[:, 5 + q % 2, h * P:(h + 1) * P], ALU.mult, ALU.add)
                            ins = dve.scalar_tensor_tensor(n0[:, q, h:h + 1], n0[:, q, h:h + 1], dc,
                                                           ps[:, 3 if q % 2 else 7, h:h + 1], ALU.mult, ALU.add)
                        ins.then_inc(s_sc, 1)


UNITS = ([(0, 0)] + [(1, r) for r in range(RES[1])], [(2, r) for r in range(RES[2])])


def sample_attention(nc, k, d):
    GH = G * H
    jobs = [(v, s, part) for v in range(2) for s in range(NS) for part in range(2)]
    with ExitStack() as ctx:
        sb = lambda n, s, dt=F32: ctx.enter_context(nc.sbuf_tensor(n, s, dt))
        ring = sb("sa_ring", [P, NR, RES[2] * H * P])
        smask = sb("sa_mask", [TS, G, P + TS])
        scT = sb("sa_scT", [P, GH, TS])
        sc = sb("sa_sc", [TS, H, G, P + TS])
        pT = sb("sa_pT", [P, GH, TS])
        pN = sb("sa_pN", [TS, GH, TS])
        mx = sb("sa_mx", [TS, H])
        nb = sb("sa_nb", [TS, H])
        den = sb("sa_den", [TS, H])
        rden = sb("sa_rden", [TS, H])
        ready = [k.sem(f"sa_ready{r}") for r in range(NR)]
        s_m, s_used, s_scT, s_tr, s_nb, s_exp, s_norm, s_pt, s_pe, s_pv, s_chain, s_new = (
            k.sem("sa_" + n) for n in ("mask", "used", "scores_taken", "scores", "max", "exp", "norm", "turned",
                                       "turned_taken", "pv", "chain", "new"))
        ps = k.ps

        def queries(t, g, s, r):
            return t[:, s * LS + r:(s + 1) * LS:RES[g]]

        with nc.Block() as block:
            @block.sync
            def _(sp):
                sp.dma_start(smask[:].rearrange("p g n -> p (g n)"), d["c_smask"]).then_inc(s_m, 16)
                for n, (v, s, part) in enumerate(jobs):
                    if n >= NR:
                        sp.wait_ge(s_used, n - NR + 1)
                    units = UNITS[part]
                    if v == 0:
                        dst = ring[:, n % NR, 0:len(units) * H * P]
                        src = d["kcacheA" if part == 0 else "kcacheB"][s]
                        sp.dma_start(dst, src).then_inc(ready[n % NR], 16)
                    else:
                        for g in sorted({g for g, _ in units}):
                            at = [u[0] for u in units].index(g)
                            dst = ring[:, n % NR, at * H * P:(at + RES[g]) * H * P].rearrange("p (r n) -> p r n", r=RES[g])
                            src = d[f"cache{g}"][s].rearrange("(j r two n) -> j r two n", r=DILATIONS[g], two=2,
                                                              n=H * P)[:, 0:RES[g], 1, :]
                            sp.dma_start(dst, src).then_inc(ready[n % NR], 16)
                for g in range(G):
                    sp.dma_start(d["kT_s"][g], k.qkS[:, (2 * g + 1) * H:(2 * g + 2) * H, :]).then_inc(s_new, 16)
                sp.dma_start(d["v_s"], k.vS[0:TS]).then_inc(s_new, 16)
                sp.wait_ge(s_new, 16 * (G + 1))

            def softmax_products(pe):
                pe.wait_ge(s_scT, 1)
                for gh in range(GH):
                    g, h = divmod(gh, H)
                    pe.transpose(ps[0:TS, 2 + g, h * P:(h + 1) * P], scT[:, gh, :], k.ident[:])
                for gh in range(GH):
                    g, h = divmod(gh, H)
                    mm = pe.matmul(ps[0:TS, 5 + gh // 8, (gh % 8) * TS:(gh % 8 + 1) * TS], k.qkS[:, 2 * g * H + h, :],
                                   k.qkS[:, (2 * g + 1) * H + h, :], start=True, stop=True)
                mm.then_inc(s_tr, 1)
                pe.wait_ge(s_norm, 1)
                for gh in range(GH):
                    g, h = divmod(gh, H)
                    pe.transpose(ps[:, gh // 8, (gh % 8) * TS:(gh % 8 + 1) * TS], sc[:, h, g, 0:P], k.ident[0:TS, 0:TS])
                    mm = pe.transpose(ps[0:TS, 2 + gh // 8, (gh % 8) * TS:(gh % 8 + 1) * TS], sc[:, h, g, P:],
                                      k.ident[0:TS, 0:TS])
                mm.then_inc(s_pt, 1)
                pe.wait_ge(s_pe, 1)
                for gh in range(GH):
                    g, h = divmod(gh, H)
                    pe.matmul(ps[:, 4 + h, 0:TS], k.vS[0:TS, g, h * P:(h + 1) * P], pN[:, gh, :],
                              start=g == 0, stop=False, skip_group_check=True)

            @block.tensor
            def _(pe):
                arrived = [0] * NR
                for n, (v, s, part) in enumerate(jobs):
                    if n == NS * 2:
                        softmax_products(pe)
                    arrived[n % NR] += 16 * (2 if v and part == 0 else 1)
                    pe.wait_ge(ready[n % NR], arrived[n % NR])
                    for u, (g, r) in enumerate(UNITS[part]):
                        for h in range(H):
                            gh = g * H + h
                            if v == 0:
                                kc = ring[:, n % NR, (u * H + h) * P:(u * H + h + 1) * P]
                                o = ps[:, gh // 8, (gh % 8) * TS:(gh % 8 + 1) * TS]
                                mm = pe.matmul(queries(o, g, s, r), kc, queries(k.qkS[:, 2 * g * H + h, :], g, s, r),
                                               start=True, stop=True)
                            else:
                                vc = ring[:, n % NR, (u * H + h) * P:(u * H + h + 1) * P]
                                last = s == NS - 1 and (g, r) == UNITS[1][-1]
                                mm = pe.matmul(queries(ps[:, 4 + h, 0:TS], g, s, r), vc, queries(pT[:, gh, :], g, s, r),
                                               start=False, stop=last, skip_group_check=True)
                    mm.then_inc(s_used, 1)

            @block.scalar
            def _(act):
                act.wait_ge(s_used, 2 * NS)
                act.activation(scT[:, 0:8, :].rearrange("p a n -> p (a n)"), ps[:, 0, :], ACT.Copy)
                act.activation(scT[:, 8:GH, :].rearrange("p a n -> p (a n)"), ps[:, 1, 0:(GH - 8) * TS],
                               ACT.Copy).then_inc(s_scT, 1)
                act.wait_ge(s_nb, 1)
                for h in range(H):
                    v = sc[:, h].rearrange("p g n -> p (g n)")
                    ins = act.activation(v, v, ACT.Exp, bias=nb[:, h:h + 1], scale=SCALE, accum_out=den[:, h:h + 1])
                ins.then_inc(s_exp, 1)
                act.wait_ge(s_pt, 1)
                for dst, b, q in ((pT, 0, P), (pN, 2, TS)):
                    act.activation(dst[:, 0:8, :].rearrange("p a n -> p (a n)"), ps[0:q, b, :], ACT.Copy)
                    ins = act.activation(dst[:, 8:GH, :].rearrange("p a n -> p (a n)"),
                                         ps[0:q, b + 1, 0:(GH - 8) * TS], ACT.Copy)
                ins.then_inc(s_pe, 1)
                act.wait_ge(s_used, 4 * NS)
                for h in range(H):
                    ins = act.activation(k.oaT[:, h, SEQ:T], ps[:, 4 + h, 0:TS], ACT.Copy)
                ins.then_inc(s_pv, 1)
                act.wait_ge(s_pv, 1)

            @block.vector
            def _(dve):
                chain = Chain(dve, s_chain)
                dve.wait_ge(s_m, 16)
                dve.wait_ge(s_tr, 1)
                for g in range(G):
                    dve.tensor_tensor(sc[:, :, g, 0:P], ps[0:TS, 2 + g, :].rearrange("p (h n) -> p h n", h=H),
                                      broadcast_mid(smask[:, g, 0:P], H, 1), ALU.add)
                    b, o = 5 + (g * H) // 8, (g * H) % 8 * TS
                    ins = dve.tensor_tensor(sc[:, :, g, P:], ps[0:TS, b, o:o + H * TS].rearrange("p (h n) -> p h n", h=H),
                                            broadcast_mid(smask[:, g, P:], H, 1), ALU.add)
                chain.step(ins)
                v = sc[:].rearrange("p h g n -> p h (g n)")
                chain.step(dve.tensor_reduce(mx[:], v, AX, ALU.max))
                dve.tensor_scalar(nb[:], mx[:], -SCALE, None, ALU.mult).then_inc(s_nb, 1)
                dve.wait_ge(s_exp, 1)
                chain.step(dve.reciprocal(rden[:], den[:]))
                dve.tensor_tensor(v, v, broadcast_mid(rden[:], G * (P + TS), 2), ALU.mult).then_inc(s_norm, 1)


def gate_projections(nc, k, d, gate):
    def take(n):
        def f(act, j, halves):
            act.activation(gate[:, H * n + j, 0:TH], halves[0], ACT.Sigmoid)
            return act.activation(gate[:, H * n + j, TH:T], halves[1], ACT.Sigmoid)
        return f
    project(nc, k, "gp", k.hT, [("feature", d["w_merge"][n], take(n)) for n in range(4)])


def merge(nc, k, d, gate):
    with ExitStack() as ctx:
        wab = ctx.enter_context(nc.sbuf_tensor("mg_w", [P, 2, H, D], F32))
        s_w, s_mm, s_t, s_add = (k.sem("mg_" + n) for n in ("w", "mm", "taken", "add"))
        ps = k.ps
        with nc.Block() as block:
            @block.sync
            def _(sp):
                sp.dma_start(wab[:, 0], d["w_a"]).then_inc(s_w, 16)
                sp.dma_start(wab[:, 1], d["w_b"]).then_inc(s_w, 16)

            @block.tensor
            def _(pe):
                pe.wait_ge(s_w, 32)
                for b in range(KD):
                    if b >= 2:
                        pe.wait_ge(s_t, 4 * (b - 1))
                    for br, src in ((0, k.hmT), (1, k.oaT)):
                        for c in range(H):
                            on = dict(start=c == 0, stop=c == H - 1)
                            wc = wab[:, br, c, b * P:(b + 1) * P]
                            pe.matmul(ps[:, 4 * (b % 2) + 2 * br, 0:TH], wc, src[:, c, 0:TH], **on)
                            mm = pe.matmul(ps[:, 4 * (b % 2) + 2 * br + 1, 0:TH], wc, src[:, c, TH:T], **on)
                    mm.then_inc(s_mm, 1)

            @block.vector
            def _(dve):
                for b in range(KD):
                    dve.wait_ge(s_mm, b + 1)
                    for br in range(2):
                        g = gate[:, br * KD + b, :]
                        bank = 4 * (b % 2) + 2 * br
                        dve.tensor_tensor(g[:, 0:TH], ps[:, bank, 0:TH], g[:, 0:TH], ALU.mult).then_inc(s_t, 1)
                        dve.tensor_tensor(g[:, TH:T], ps[:, bank + 1, 0:TH], g[:, TH:T], ALU.mult).then_inc(s_t, 1)
                    dve.wait_ge(s_t, 4 * (b + 1))
                    dve.tensor_tensor(k.hT[:, b, :], gate[:, b, :], gate[:, KD + b, :], ALU.add).then_inc(s_add, 1)
                dve.wait_ge(s_add, KD)


def output_projection(nc, k, d, e):
    with ExitStack() as ctx:
        sb = lambda n, s, dt=F32: ctx.enter_context(nc.sbuf_tensor(n, s, dt))
        w = sb("op_w", [P, 2, KD, CHUNK])
        rows = sb("op_rows", [P, 2, 3, D])
        junk = sb("op_junk", [P, D])
        ss = sb("op_ss", [P, 2, NCH, 2])
        ms = sb("op_ms", [P, 2, NCH])
        rt = sb("op_rt", [P, 2, NCH])
        rs = sb("op_rs", [P, 2, NCH])
        y = sb("op_y", [P, 2, D])
        s_w, s_r, s_x, s_mm, s_sq, s_ms, s_rt, s_y, s_x1, s_h2, s_tr, s_tt, s_chain, s_act, s_sc = (
            k.sem("op_" + n) for n in ("w", "rows", "x", "mm", "square", "ms", "root", "taken", "x1", "h2", "turned",
                                       "turned_taken", "chain", "act", "scratch"))
        ps = k.ps
        with nc.Block() as block:
            @block.sync
            def _(sp):
                for n in range(2):
                    sp.dma_start(w[:, n], d["w_out"][n]).then_inc(s_w, 16)
                sp.dma_start(e.x1[:, 0:PT, :], d["x_prompt"].rearrange("(t p) n -> p t n", p=P)).then_inc(s_x, 16)
                sp.dma_start(e.x1[0:TS, PT, :], d["x_sample"]).then_inc(s_x, 16)
                for j in range(3):
                    sp.dma_start(rows[:, 0, j, :], d["rows"][j][0].partition_broadcast(P)).then_inc(s_r, 16)
                    for s in range(NS):
                        sp.dma_start(rows[s * LS:(s + 1) * LS, 1, j, :],
                                     d["rows"][j][1 + s].partition_broadcast(LS)).then_inc(s_r, 16)

            @block.tensor
            def _(pe):
                def product(i):
                    r = tile_rows(i)
                    if i >= 2:
                        pe.wait_ge(s_y, i - 1)
                    for n in range(2):
                        for c in range(KD):
                            mm = pe.matmul(ps[0:r, 2 * (i % 2) + n, :], k.hT[:, c, tile_cols(i)], w[:, n, c, :],
                                           start=c == 0, stop=c == KD - 1)
                    mm.then_inc(s_mm, 1)

                def turn(i):
                    r = tile_rows(i)
                    pe.wait_ge(s_h2, i + 1)
                    if i >= 2:
                        pe.wait_ge(s_tt, i - 1)
                    for c in range(KD):
                        mm = pe.transpose(ps[:, 4 + 2 * (i % 2) + c // 4, (c % 4) * P:(c % 4) * P + r],
                                          e.h2[0:r, i, c * P:(c + 1) * P], k.ident[0:r, 0:r])
                    mm.then_inc(s_tr, 1)

                pe.wait_ge(s_w, 32)
                for i in range(NCH):
                    product(i)
                    if i >= 1:
                        turn(i - 1)
                turn(NCH - 1)

            @block.scalar
            def _(act):
                chain = Chain(act, s_act)
                for i in range(NCH):
                    r = tile_rows(i)
                    act.wait_ge(s_mm, i + 1)
                    for n in range(2):
                        chain.step(act.activation(junk[0:r, 0:CHUNK], ps[0:r, 2 * (i % 2) + n, :], ACT.Square,
                                                  accum_out=ss[0:r, 0, i, n:n + 1]))
                    act.sem_inc(s_sq, 1)
                    act.wait_ge(s_ms, 2 * i + 1)
                    act.activation(rt[0:r, 0, i:i + 1], ms[0:r, 0, i:i + 1], ACT.Sqrt).then_inc(s_rt, 1)
                    act.wait_ge(s_x1, i + 1)
                    act.activation(junk[0:r], e.x1[0:r, i, :], ACT.Square, accum_out=ss[0:r, 1, i, 0:1]).then_inc(s_sq, 1)
                    act.wait_ge(s_ms, 2 * i + 2)
                    act.activation(rt[0:r, 1, i:i + 1], ms[0:r, 1, i:i + 1], ACT.Sqrt).then_inc(s_rt, 1)
                    act.wait_ge(s_tr, i + 1)
                    src = ps[:, 4 + 2 * (i % 2):6 + 2 * (i % 2), :].rearrange("p b (c t) -> p (b c) t", t=P)
                    act.activation(e.h2T[:, :, tile_cols(i)], src[:, :, 0:r], ACT.Copy).then_inc(s_tt, 1)
                act.wait_ge(s_tt, NCH)

            @block.vector
            def _(dve):
                chain = Chain(dve, s_chain)
                dve.wait_ge(s_x, 32)
                dve.wait_ge(s_r, 16 * 3 * (1 + NS))
                for i in range(NCH):
                    r, kind = tile_rows(i), int(i == PT)
                    dve.wait_ge(s_sq, 2 * i + 1)
                    chain.step(dve.tensor_tensor(ss[0:r, 0, i, 0:1], ss[0:r, 0, i, 0:1], ss[0:r, 0, i, 1:2], ALU.add))
                    dve.tensor_scalar(ms[0:r, 0, i:i + 1], ss[0:r, 0, i, 0:1], 1.0 / D, EPS, ALU.mult,
                                      ALU.add).then_inc(s_ms, 1)
                    dve.wait_ge(s_rt, 2 * i + 1)
                    chain.step(dve.reciprocal(rs[0:r, 0, i:i + 1], rt[0:r, 0, i:i + 1]))
                    for n in range(2):
                        o = slice(n * CHUNK, (n + 1) * CHUNK)
                        ins = dve.scalar_tensor_tensor(y[0:r, 0, o], ps[0:r, 2 * (i % 2) + n, :], rs[0:r, 0, i:i + 1],
                                                       rows[0:r, kind, 0, o], ALU.mult, ALU.mult)
                    ins.then_inc(s_y, 1)
                    dve.wait_ge(s_y, i + 1)
                    dve.tensor_tensor(e.x1[0:r, i, :], e.x1[0:r, i, :], y[0:r, 0, :], ALU.add).then_inc(s_x1, 1)
                    dve.wait_ge(s_sq, 2 * i + 2)
                    dve.tensor_scalar(ms[0:r, 1, i:i + 1], ss[0:r, 1, i, 0:1], 1.0 / D, EPS, ALU.mult,
                                      ALU.add).then_inc(s_ms, 1)
                    dve.wait_ge(s_rt, 2 * i + 2)
                    chain.step(dve.reciprocal(rs[0:r, 1, i:i + 1], rt[0:r, 1, i:i + 1]))
                    chain.step(dve.scalar_tensor_tensor(y[0:r, 1, :], e.x1[0:r, i, :], rs[0:r, 1, i:i + 1],
                                                        rows[0:r, kind, 1, :], ALU.mult, ALU.mult))
                    dve.tensor_tensor(e.h2[0:r, i, :], y[0:r, 1, :], rows[0:r, kind, 2, :], ALU.add).then_inc(s_h2, 1)


def query_projections(nc, k, d, e):
    def take(n):
        def f(act, j, halves):
            act.activation(e.qT[:, H * n + j, 0:TH], halves[0], ACT.Copy)
            return act.activation(e.qT[:, H * n + j, TH:T], halves[1], ACT.Copy)
        return f
    project(nc, k, "qp", e.h2T, [("feature", d["peer_wq"][n], take(n)) for n in range(4)])


def routed_beside(i, h):
    out = [(0, h + 1)] if i == 0 and h + 1 < PH else []
    if i + 1 < NCH and h < heads_of(i + 1):
        out.append((i + 1, h))
    return out


ROUTED = [(0, 0)] + [x for i in range(NCH) for h in range(heads_of(i)) for x in routed_beside(i, h)]
RING = 8
BATCH = 2


def peer(nc, k, d, e):
    with ExitStack() as ctx:
        sb = lambda n, s, dt=F32: ctx.enter_context(nc.sbuf_tensor(n, s, dt))
        ring = sb("pr_ring", [P, RING, 2 * D])
        keysT = sb("pr_keysT", [P, 2, NKEYS])
        sc = sb("pr_sc", [P, 2, 2 * PH, NKEYS])
        packed = sb("pr_packed", [P, PH, P])
        rest = sb("pr_rest", [P, NKEYS])
        val = sb("pr_val", [P, 2, TOPK])
        ind = sb("pr_ind", [P, 2, TOPK], U32)
        indf = sb("pr_indf", [P, 2, TOPK])
        cand = sb("pr_cand", [P, TOPK, TOPK])
        crest = sb("pr_crest", [P, TOPK, TOPK])
        top = sb("pr_top", [P, TOPK])
        pos = sb("pr_pos", [P, TOPK], U32)
        part = sb("pr_part", [P, 2, TOPK], U32)
        partf = sb("pr_partf", [P, 2, TOPK])
        hot = sb("pr_hot", [P, 2, TOPK, TOPK])
        pick = sb("pr_pick", [P, 2, TOPK])
        ntop = sb("pr_ntop", [P, 1])
        ex = sb("pr_ex", [P, TOPK])
        exs = sb("pr_exs", [P, 1])
        rex = sb("pr_rex", [P, 1])
        idx = sb("pr_idx", [P, 2, SLOTS], U32)
        wgt = sb("pr_wgt", [P, 2, SLOTS])
        junk = sb("pr_junk", [P, BATCH, D])
        dots = sb("pr_dots", [P, RING])
        gel = sb("pr_gel", [P, RING])
        diag = sb("pr_diag", [P, RING, P])
        gate2 = sb("pr_gate2", [P, 2, D])
        fj = sb("pr_fj", [P, D])
        fy = sb("pr_fy", [P, D])
        fss = sb("pr_fss", [P, 2])
        fms = sb("pr_fms", [P, 1])
        frt = sb("pr_frt", [P, 1])
        frs = sb("pr_frs", [P, 1])
        arrived = [k.sem(f"pr_row{r}") for r in range(RING)]
        s_pk, s_in, s_sc, s_sct, s_nt, s_ex, s_idx, s_dot, s_gel, s_dg, s_v, s_f, s_fsq, s_fms, s_frt, s_ft, s_y, s_out, s_chain, s_act = (
            k.sem("pr_" + n) for n in ("packed", "in", "scores", "scores_taken", "top", "exp", "routed", "dots", "gelu", "diag",
                                       "values", "sum", "sum_square", "sum_ms", "sum_root", "sum_taken", "y", "out",
                                       "chain", "act"))
        ps = k.ps
        order = list(range(NCH))
        routed = {x: n + 1 for n, x in enumerate(ROUTED)}
        with nc.Block() as block:
            @block.sync
            def _(sp):
                sp.dma_start(keysT[:], d["keysT"]).then_inc(s_in, 16)
                sp.dma_start(e.h2[TS:P, PT, :], e.h2[0:TS, PT, :]).then_inc(s_in, 16)
                sp.dma_start(gate2[:, 0, :], d["rows"][3][0].partition_broadcast(P)).then_inc(s_in, 16)
                for s in range(NS):
                    sp.dma_start(gate2[s * LS:(s + 1) * LS, 1, :],
                                 d["rows"][3][1 + s].partition_broadcast(LS)).then_inc(s_in, 16)
                for i in order:
                    sp.wait_ge(s_y, i + 1)
                    if i < PT:
                        sp.dma_start(d["y_p"][i * P:(i + 1) * P, :], e.x1[:, i, :]).then_inc(s_out, 16)
                    else:
                        sp.dma_start(d["y_s"], e.x1[0:TS, i, :]).then_inc(s_out, 16)
                sp.wait_ge(s_out, 16 * NCH)
                sp.wait_ge(k.s_roll, 16 * k.n_rolls)

            @block.gpsimd
            def _(pool):
                for half in range(2):
                    ins = pool.tensor_copy(packed[:, :, half * TS:(half + 1) * TS],
                                           e.qT[:, half * PH:(half + 1) * PH, SEQ:T])
                ins.then_inc(s_pk, 1)
                for i in order:
                    for q in range(heads_of(i) * TOPK):
                        n = i * SLOTS + q
                        if q % TOPK == 0:
                            pool.wait_ge(s_idx, routed[i, q // TOPK])
                        if n >= RING:
                            pool.wait_ge(s_v, n - RING + 1)
                        pool.indirect_dma_start(ring[:, n % RING, :], None, d["uv"],
                                                bass.IndirectOffsetOnAxis(ap=idx[:, i % 2, q:q + 1], axis=0)
                                                ).then_inc(arrived[n % RING], 16)

            @block.tensor
            def _(pe):
                def scores(i):
                    if i >= 1:
                        pe.wait_ge(s_sct, i)
                    for b in range(2 * heads_of(i)):
                        q = e.qT[:, b, tile_cols(i)] if i < PT else packed[:, b, :]
                        mm = pe.matmul(ps[:, b // 4, (b % 4) * P:(b % 4 + 1) * P], q,
                                       keysT[:, b % 2, :], start=True, stop=True)
                    mm.then_inc(s_sc, 1)

                pe.wait_ge(s_in, 16 * (3 + NS))
                pe.wait_ge(s_pk, 1)
                scores(0)
                for i in order:
                    r = tile_rows(i)
                    if i + 1 < NCH:
                        scores(i + 1)
                    if i >= 2:
                        pe.wait_ge(s_ft, i - 1)
                    last = heads_of(i) * TOPK - 1
                    for q in range(last + 1):
                        n = i * SLOTS + q
                        pe.wait_ge(s_dg, n + 1)
                        for half in range(2):
                            o = D + half * CHUNK
                            mm = pe.matmul(ps[0:r, 4 + 2 * (i % 2) + half, :], diag[:, n % RING, 0:r],
                                           ring[:, n % RING, o:o + CHUNK], start=q == 0, stop=q == last)
                        mm.then_inc(s_v, 1)

            @block.scalar
            def _(act):
                chain = Chain(act, s_act)

                def scores_taken(i):
                    act.wait_ge(s_sc, i + 1)
                    if i >= 2:
                        act.wait_ge(s_idx, routed[i - 2, PH - 1])
                    for b in range(heads_of(i) // 2):
                        ins = act.activation(sc[:, i % 2, 4 * b:4 * b + 4, :].rearrange("p a n -> p (a n)"),
                                             ps[:, b, :], ACT.Copy)
                    ins.then_inc(s_sct, 1)

                def route_exp(i, h):
                    act.wait_ge(s_nt, routed[i, h])
                    act.activation(ex[:], top[:], ACT.Exp, bias=ntop[:], accum_out=exs[:]).then_inc(s_ex, 1)

                def finish(i):
                    r = tile_rows(i)
                    act.wait_ge(s_v, i * SLOTS + heads_of(i) * TOPK)
                    if i >= 1:
                        act.wait_ge(s_y, i)
                    for half in range(2):
                        chain.step(act.activation(fj[0:r, 0:CHUNK], ps[0:r, 4 + 2 * (i % 2) + half, :], ACT.Square,
                                                  accum_out=fss[0:r, half:half + 1]))
                    act.sem_inc(s_fsq, 1)
                    act.wait_ge(s_fms, i + 1)
                    act.activation(frt[0:r], fms[0:r], ACT.Sqrt).then_inc(s_frt, 1)

                scores_taken(0)
                route_exp(0, 0)
                for i in order:
                    for h in range(heads_of(i)):
                        for t, g in routed_beside(i, h):
                            if g == 0:
                                scores_taken(t)
                            route_exp(t, g)
                        for q in range(h * TOPK, (h + 1) * TOPK, BATCH):
                            n = i * SLOTS + q
                            o = n % RING
                            act.wait_ge(s_dot, n // BATCH + 1)
                            act.activation(gel[:, o:o + BATCH], dots[:, o:o + BATCH], ACT.Gelu).then_inc(s_gel, 1)
                    finish(i)

            @block.vector
            def _(dve):
                chain = Chain(dve, s_chain)

                def top16(r, values, rest_, out, index):
                    chain.step(dve.max(out[0:r, 0:8], values))
                    dve.max_index(index[0:r, 0:8], out[0:r, 0:8], values)
                    chain.step(dve.match_replace(rest_, out[0:r, 0:8], values, NEG))
                    chain.step(dve.max(out[0:r, 8:16], rest_))
                    return dve.max_index(index[0:r, 8:16], out[0:r, 8:16], rest_)

                def route(i, h):
                    r, buf = P, i % 2
                    if h == 0:
                        dve.wait_ge(s_sct, i + 1)
                        if i >= 2:
                            dve.wait_ge(s_v, (i - 1) * SLOTS)
                    for half in range(2):
                        chain.step(top16(r, sc[:, i % 2, 2 * h + half, :], rest[:], val[:, half, :], ind[:, half, :]))
                    dve.tensor_copy(indf[0:r], ind[0:r])
                    chain.step(dve.tensor_tensor(cand[0:r], broadcast_mid(val[0:r, 0, :], TOPK, 2),
                                                 broadcast_mid(val[0:r, 1, :], TOPK, 1), ALU.add))
                    flat = cand[0:r].rearrange("p a b -> p (a b)")
                    chain.step(top16(r, flat, crest[0:r].rearrange("p a b -> p (a b)"), top[:], pos[:]))
                    dve.tensor_scalar(ntop[0:r], top[0:r, 0:1], -1.0, None, ALU.mult).then_inc(s_nt, 1)
                    dve.tensor_scalar(part[0:r, 0, :], pos[0:r], 4, None, ALU.logical_shift_right)
                    chain.step(dve.tensor_scalar(part[0:r, 1, :], pos[0:r], TOPK - 1, None, ALU.bitwise_and))
                    chain.step(dve.tensor_copy(partf[0:r], part[0:r]))
                    for half in range(2):
                        ins = dve.tensor_tensor(hot[0:r, half], broadcast_mid(partf[0:r, half, :], TOPK, 2),
                                                broadcast_mid(k.iota[0:r], TOPK, 1), ALU.is_equal)
                    chain.step(ins)
                    for half in range(2):
                        ins = dve.tensor_tensor(hot[0:r, half], hot[0:r, half],
                                                broadcast_mid(indf[0:r, half, :], TOPK, 1), ALU.mult)
                    chain.step(ins)
                    chain.step(dve.tensor_reduce(pick[0:r], hot[0:r], AX, ALU.add))
                    o = slice(h * TOPK, (h + 1) * TOPK)
                    dve.scalar_tensor_tensor(idx[0:r, buf, o], pick[0:r, 0, :], float(NKEYS), pick[0:r, 1, :],
                                             ALU.mult, ALU.add)
                    dve.wait_ge(s_ex, routed[i, h])
                    chain.step(dve.reciprocal(rex[0:r], exs[0:r]))
                    dve.tensor_scalar(wgt[0:r, buf, o], ex[0:r], rex[0:r], None, ALU.mult).then_inc(s_idx, 1)
                    dve.wait_ge(s_idx, routed[i, h])

                def dots_of(i, q):
                    if i or q:
                        dve.wait_ge(s_dot, (i * SLOTS + q) // BATCH)
                    for b in range(BATCH):
                        n = i * SLOTS + q + b
                        dve.wait_ge(arrived[n % RING], 16 * (n // RING + 1))
                        ins = dve.tensor_tensor_reduce(junk[:, b], ring[:, n % RING, 0:D], e.h2[:, i, :], 1.0, 0.0,
                                                       ALU.mult, ALU.add, dots[:, n % RING:n % RING + 1])
                        if b == BATCH - 1:
                            ins.then_inc(s_dot, 1)

                def diags_of(i, q):
                    r = tile_rows(i)
                    n = i * SLOTS + q
                    dve.wait_ge(s_gel, n // BATCH + 1)
                    for b in range(BATCH):
                        o = (n + b) % RING
                        dve.tensor_scalar(diag[:, o, 0:r], k.ident[:] if i < PT else k.fold[:], gel[:, o:o + 1],
                                          wgt[:, i % 2, q + b:q + b + 1], ALU.mult, ALU.mult).then_inc(s_dg, 1)

                def finish(i):
                    r, kind = tile_rows(i), int(i == PT)
                    dve.wait_ge(s_fsq, i + 1)
                    chain.step(dve.tensor_tensor(fss[0:r, 0:1], fss[0:r, 0:1], fss[0:r, 1:2], ALU.add))
                    dve.tensor_scalar(fms[0:r], fss[0:r, 0:1], 1.0 / D, EPS, ALU.mult, ALU.add).then_inc(s_fms, 1)
                    dve.wait_ge(s_frt, i + 1)
                    chain.step(dve.reciprocal(frs[0:r], frt[0:r]))
                    for half in range(2):
                        o = slice(half * CHUNK, (half + 1) * CHUNK)
                        ins = dve.scalar_tensor_tensor(fy[0:r, o], ps[0:r, 4 + 2 * (i % 2) + half, :], frs[0:r],
                                                       gate2[0:r, kind, o], ALU.mult, ALU.mult)
                    ins.then_inc(s_ft, 1)
                    dve.wait_ge(s_ft, i + 1)
                    dve.tensor_tensor(e.x1[0:r, i, :], e.x1[0:r, i, :], fy[0:r], ALU.add).then_inc(s_y, 1)

                dve.wait_ge(s_in, 16 * (3 + NS))
                route(0, 0)
                for i in order:
                    for h in range(heads_of(i)):
                        for t, g in routed_beside(i, h):
                            route(t, g)
                        for q in range(h * TOPK, (h + 1) * TOPK, BATCH):
                            dots_of(i, q)
                            if q:
                                diags_of(i, q - BATCH)
                    diags_of(i, heads_of(i) * TOPK - BATCH)
                    finish(i)


def build(nc, d):
    with ExitStack() as ctx:
        sb = lambda n, s, dt=F32, c=ctx: c.enter_context(nc.sbuf_tensor(n, s, dt))
        k = Shared()
        k.sem = lambda n: ctx.enter_context(nc.semaphore(n))
        k.ps = ctx.enter_context(nc.psum_tensor("ps", [P, 8, 512], F32))
        k.ident = sb("ident", [P, P])
        k.sel = sb("sel", [H, H * P])
        k.block = sb("block", [TS, NS])
        k.fold = sb("fold", [P, TS])
        k.iota = sb("iota", [P, TOPK])
        k.shift1 = sb("shift1", [P, KD, NC])
        k.scale1 = sb("scale1", [P, KD, NC])
        k.s_roll = k.sem("rolled")
        k.rolls = roll_pieces(d)
        k.n_rolls = len(k.rolls)
        modulation(nc, k, d)
        trunk = sb("trunk", [P, 2 * KD, T])
        k.hT, k.oaT, k.hmT = trunk[:, 0:KD, :], trunk[:, KD:KD + H, :], trunk[:, KD + H:, :]
        normalised_input(nc, k, d)
        with ExitStack() as att:
            k.qkS = sb("qkS", [P, 2 * G * H, TS], F32, att)
            k.vS = sb("vS", [TS, G, H * P], F32, att)
            with ExitStack() as pa:
                a = Shared()
                a.qk = sb("a_qk", [P, 2 * G * H, SEQ], F32, pa)
                a.v = sb("a_v", [P, PT, G, H * P], F32, pa)
                attention_projections(nc, k, d, a)
                prompt_attention(nc, k, d, a)
            sample_attention(nc, k, d)
        with ExitStack() as ml:
            ms = lambda n, s: sb(n, s, F32, ml)
            m = Shared()
            m.raw, m.rawS = ms("m_raw", [P, 2 * H, CW - 1 + SEQ]), ms("m_rawS", [P, 2 * H, NS * (CW - 1 + LS)])
            m.v, m.o, m.qk = ms("m_v", [P, NCH, H * P]), ms("m_o", [P, NCH, H * P]), ms("m_qk", [P, 2 * H, T])
            m.rows, m.M, m.decay = ms("m_rows", [H, 4, T]), ms("m_M", [H, T]), ms("m_decay", [H, PT + NS])
            m.cols, m.dcols, m.ones = ms("m_cols", [P, NCH, 4, H]), ms("m_dcols", [P, H, PT + NS]), ms("m_ones", [P, 1])
            mlstm_projections(nc, k, d, m)
            conv_and_gates(nc, k, d, m)
            mlstm(nc, k, d, m)
        with ExitStack() as mg:
            gate = sb("gate", [P, 2 * KD, T], F32, mg)
            gate_projections(nc, k, d, gate)
            merge(nc, k, d, gate)
        e = Shared()
        e.x1, e.h2, e.qT = sb("x1", [P, NCH, D]), sb("h2", [P, NCH, D]), trunk
        with ExitStack() as mid:
            e.h2T = sb("h2T", [P, KD, T], F32, mid)
            output_projection(nc, k, d, e)
            query_projections(nc, k, d, e)
        peer(nc, k, d, e)


def kernel(**inputs):
    import concourse.bacc as bacc
    from concourse.bass_utils import run_bass_kernel_spmd

    a = {n: np.asarray(x) for n, x in inputs.items()}
    W = H * P
    w_in = a["w_in"][0]
    at = np.cumsum([0, 2 * W, W, W, H, H] + [W] * (3 * G) + [D, D]).tolist()

    def by_row(w):
        return w.reshape(-1, P, w.shape[1]).transpose(1, 0, 2)

    def chunks(w):
        return np.stack([by_row(w[:, o:o + CHUNK]) for o in range(0, w.shape[1], CHUNK)])

    def part(i, n=1):
        return w_in[:, at[i]:at[i + n]]

    attn = [part(5 + 3 * g + j) for g in range(G) for j in range(2)]
    ins = {
        "cT": by_row(np.concatenate([a["c_prompt"], a["c_sample"]]).T),
        "w_ada": chunks(a["w_ada"][0]), "b_ada": a["b_ada"][0],
        "g_pre1": a["g_pre1"][0].reshape(KD, P).T, "g_post1": a["g_post1"][0], "g_pre2": a["g_pre2"][0],
        "g_post2": a["g_post2"][0],
        "x_prompt": a["x_prompt"][0], "x_sample": a["x_sample"].reshape(TS, D),
        "w_attn_qk": np.stack([by_row(w) for w in attn]),
        "w_attn_v": np.stack([by_row(part(7 + 3 * g)) for g in range(G)]),
        "w_qk": chunks(part(0)), "w_mv": by_row(part(1)), "w_mo": by_row(part(2)),
        "w_gates": by_row(part(3, 2)), "b_gates": np.stack([a["b_igate"][0], a["b_fgate"][0]], 1),
        "w_merge": chunks(part(14, 2)),
        "conv_w": np.concatenate([a["conv_w"][0], a["conv_b"]]).reshape(CW + 1, 2 * H, P).transpose(2, 1, 0),
        "stateT": a["state_conv"][0].reshape(NS, CW - 1, 2 * H, P).transpose(3, 2, 0, 1),
        "m0": a["state_mlstm_m"][0].T,
        "C0": a["state_mlstm_C"][0].transpose(2, 0, 1, 3), "n0": a["state_mlstm_n"][0].transpose(2, 0, 1),
        "mh_norm_g": a["mh_norm_g"][0].reshape(H, P).T,
        "w_a": by_row(a["w_a"][0]), "w_b": by_row(a["w_b"][0]), "w_out": chunks(a["w_out"][0]),
        "peer_wq": chunks(a["peer_wq"][0]),
        "keysT": np.stack([a["peer_k1"][0].T, a["peer_k2"][0].T], 1),
        "uv": np.concatenate([a["peer_u"][0], a["peer_v"][0]], 1),
    }
    kc = []
    for g in range(G):
        c = a[f"cache_win{g}_kv"][0]
        ins[f"cache{g}"] = c.reshape(NS, -1)
        keys = c[:, :, 0].reshape(NS, P, DILATIONS[g], H, P)[:, :, :RES[g]]
        kc.append(keys.transpose(0, 4, 2, 3, 1).reshape(NS, P, -1))
    ins["kcacheA"] = np.concatenate(kc[:2], 2)
    ins["kcacheB"] = kc[2]
    ins.update(constants())
    ins = {n: np.ascontiguousarray(x) for n, x in ins.items()}
    outs = {
        "y_p": (SEQ, D), "y_s": (TS, D), "kT_p": (G, P, H, SEQ), "v_p": (G, P, PT, W), "kT_s": (G, P, H, TS),
        "v_s": (TS, G, W), "C_p": (P, H, P), "n_p": (P, H), "C_s": (P, NS, H, P), "n_s": (P, NS, H),
        "m_new": (H, 1 + NS), "conv_p": (P, 2 * H, CW - 1), "conv_s": (P, 2 * H, NS, CW - 1),
        **{f"win{g}_s": (NS, (WINDOWS[g] - LS) * D) for g in range(G)},
    }
    nc = bacc.Bacc("TRN2", target_bir_lowering=False, num_devices=1)
    d = {n: nc.dram_tensor("in_" + n, x.shape, mybir.dt.from_np(x.dtype), kind="ExternalInput").ap()
         for n, x in ins.items()}
    d.update({n: nc.dram_tensor("out_" + n, s, F32, kind="ExternalOutput").ap() for n, s in outs.items()})
    d["rows"] = nc.dram_tensor("rows", (4, NC, D), F32, kind="Internal").ap()
    build(nc, d)
    res = run_bass_kernel_spmd(nc, [{"in_" + n: x for n, x in ins.items()}], core_ids=[0]).results[0]
    r = {n: np.asarray(res["out_" + n]).reshape(s) for n, s in outs.items()}

    win_p, win_s = [], []
    for g in range(G):
        keys = r["kT_p"][g].transpose(2, 1, 0)
        vals = r["v_p"][g].transpose(1, 0, 2).reshape(SEQ, H, P)
        keep = min(WINDOWS[g], SEQ)
        win_p.append(np.stack([keys, vals], 1)[SEQ - keep:][None, None])
        nk = r["kT_s"][g].transpose(2, 1, 0).reshape(NS, LS, H, P)
        nv = r["v_s"][:, g].reshape(NS, LS, H, P)
        old = r[f"win{g}_s"].reshape(NS, WINDOWS[g] - LS, 2, H, P)
        win_s.append(np.concatenate([old, np.stack([nk, nv], 2)], 1)[None])
    C_s = r["C_s"].transpose(1, 2, 0, 3)[None]
    return (r["y_p"][None], r["y_s"].reshape(NS, LS, D), *win_p,
            r["C_p"].transpose(1, 0, 2)[None, None], r["n_p"].T[None, None], r["m_new"][:, 0][None, None],
            r["conv_p"].transpose(2, 1, 0).reshape(1, 1, CW - 1, 2 * W), *win_s,
            C_s, r["n_s"].transpose(1, 2, 0)[None], r["m_new"][:, 1:].T[None],
            r["conv_s"].transpose(2, 3, 1, 0).reshape(1, NS, CW - 1, 2 * W))
```

```python
from contextlib import ExitStack

import numpy as np

import concourse.bass as bass
from concourse import mybir

F32 = mybir.dt.float32
U32 = mybir.dt.uint32
ALU = mybir.AluOpType
ACT = mybir.ActivationFunctionType
AX = mybir.AxisListType.X

P = 128
D = 1024
KD = D // P
SEQ = 512
PT = SEQ // P
NS, LS = 8, 8
TS = NS * LS
T = SEQ + TS
TH = T // 2
H = 4
G = 3
WINDOWS = (128, 512, 2048)
DILATIONS = (1, 4, 16)
RES = (1, 4, 8)
CW = 4
PH = 8
TOPK = 16
NKEYS = 128
SLOTS = PH * TOPK
EPS = 1e-6
SCALE = float(P) ** -0.5
NEG = -1e30
NC = NS + 1
CHUNK = 512
NR = 3
NCH = PT + 1


def tile_rows(i):
    return P if i < PT else TS


def heads_of(i):
    return PH if i < PT else PH // 2


def tile_cols(i):
    return slice(i * P, i * P + tile_rows(i))


def key_cols(i):
    own = (i + 1) * P
    band = min(i, 1) * P
    return [(0, own - P - band, P + band, 0), (1, 0, own, P + band), (2, 0, own, P + band + own)]


MASK_AT = np.cumsum([0] + [sum(n for _, _, n, _ in key_cols(i)) for i in range(PT)]).tolist()
NKMAX = MASK_AT[PT] - MASK_AT[PT - 1]


def constants():
    t = np.arange(P)[:, None]
    masks = np.zeros((P, MASK_AT[PT]), np.float32)
    for i in range(PT):
        for g, first, n, at in key_cols(i):
            dist = (i * P + t) - (first + np.arange(n)[None, :])
            ok = (dist >= 0) & (dist <= WINDOWS[g]) & (dist % DILATIONS[g] == 0)
            masks[:, MASK_AT[i] + at:MASK_AT[i] + at + n] = np.where(ok, 0.0, NEG)
    tok = np.arange(TS)
    seq, pos = tok // LS, tok % LS
    smask = np.zeros((TS, G, P + TS), np.float32)
    for g in range(G):
        r = pos % RES[g]
        kpos = DILATIONS[g] * np.arange(P)[None, :] + r[:, None]
        old = kpos >= pos[:, None]
        dist = pos[:, None] - pos[None, :]
        new = (seq[:, None] == seq[None, :]) & (dist >= 0) & (dist % DILATIONS[g] == 0)
        smask[:, g] = np.where(np.concatenate([old, new], 1), 0.0, NEG)
    s = np.arange(P)[:, None]
    tri = np.where(s <= np.arange(P)[None, :], 0.0, NEG)
    stri = np.full((P, TS), NEG)
    stri[:TS] = np.where((seq[:, None] == seq[None, :]) & (tok[:, None] <= tok[None, :]), 0.0, NEG)
    carry = np.ones(T)
    carry[0:SEQ:P] = 0.0
    carry[SEQ::LS] = 0.0
    restart = np.zeros(T)
    restart[SEQ::LS] = NEG
    sel = np.zeros((H, H, P))
    for h in range(H):
        sel[h, h] = 1.0
    f = lambda a: np.ascontiguousarray(a, dtype=np.float32)
    return {
        "c_ident": f(np.eye(P)), "c_masks": masks, "c_smask": f(smask.reshape(TS, -1)),
        "c_tri": f(tri), "c_stri": f(stri), "c_carry": f(np.tile(carry, (H, 1))),
        "c_restart": f(np.tile(restart, (H, 1))), "c_sel": f(sel.reshape(H, H * P)),
        "c_block": f((seq[:, None] == np.arange(NS)[None, :])),
        "c_fold": f(np.tile(np.eye(TS), (P // TS, 1))),
        "c_iota": f(np.tile(np.arange(TOPK), (P, 1))),
    }


def broadcast_mid(ap, n, at):
    dims = [list(x) for x in ap.ap]
    return bass.AP(ap.tensor, ap.offset, dims[:at] + [[0, n]] + dims[at:])


class Shared:
    pass


def roll_pieces(d):
    out = []
    for g in range(G):
        w, n = WINDOWS[g], max(1, WINDOWS[g] // 256)
        size = (w - LS) * D // n
        for s in range(NS):
            for c in range(n):
                at = c * size
                out.append((d[f"win{g}_s"][s, at:at + size].rearrange("(a n) -> a n", a=16),
                            d[f"cache{g}"][s, LS * D + at:LS * D + at + size].rearrange("(a n) -> a n", a=16)))
    return out


class Chain:

    def __init__(self, eng, sem):
        self.eng, self.sem, self.n = eng, sem, 0

    def step(self, ins):
        self.n += 1
        ins.then_inc(self.sem, 1)
        self.eng.wait_ge(self.sem, self.n)


def modulation(nc, k, d, n):
    NCK = 6 * D // CHUNK
    NORM_AT = 5
    with ExitStack() as ctx:
        sb = lambda n, s, dt=F32: ctx.enter_context(nc.sbuf_tensor(n, s, dt))
        wring = sb("ada_ring", [P, NR, KD, CHUNK])
        cT = sb("ada_cT", [P, KD, NC])
        cs = sb("ada_cs", [P, KD, NC])
        mod = sb("ada_mod", [NC, 6, D])
        bias = sb("ada_bias", [NC, 6, D])
        grow = sb("ada_grow", [NC, 3, D])
        gcol = sb("ada_gcol", [P, KD])
        junk = sb("ada_junk", [P, D])
        ms = sb("ada_ms", [P, NCH])
        rt = sb("ada_rt", [P, NCH])
        ready = [k.sem(f"ada_w_ready{r}") for r in range(NR)]
        s_c, s_b, s_silu, s_mm, s_add, s_tr, s_rows, s_chain, s_out, s_const, s_x, s_sq, s_ms, s_rt = (
            k.sem("ada_" + name) for name in ("c", "bias", "silu", "mm", "add", "tr", "rows", "chain", "out", "const",
                                              "x", "sq", "ms", "rt"))
        ps = k.ps
        with nc.Block() as block:
            @block.sync
            def _(sp):
                sp.dma_start(cT[:], d["cT"]).then_inc(s_c, 16)
                for w in range(NCK):
                    if w >= NR:
                        sp.wait_ge(s_mm, w - NR + 1)
                    sp.dma_start(wring[:, w % NR], d["w_ada"][w]).then_inc(ready[w % NR], 16)
                for j in range(4):
                    src, done = ((2, 1), (4, 2), (3, 2), (5, 3))[j]
                    sp.wait_ge(s_rows, done)
                    sp.dma_start(d["rows"][j], mod[:, src, :]).then_inc(s_out, 16)
                sp.wait_ge(s_out, 64)

            @block.scalar
            def _(act):
                for dst, src in ((k.ident, "c_ident"), (k.sel, "c_sel"), (k.block, "c_block"), (k.fold, "c_fold"),
                                 (k.iota, "c_iota"), (gcol, "g_pre1")):
                    act.dma_start(dst[:], d[src]).then_inc(s_const, 16)
                act.dma_start(bias[:].rearrange("p a n -> p (a n)"), d["b_ada"].partition_broadcast(NC)).then_inc(s_b, 16)
                for j, name in enumerate(("g_post1", "g_pre2", "g_post2")):
                    act.dma_start(grow[:, j], d[name].partition_broadcast(NC)).then_inc(s_b, 16)
                act.dma_start(n.x[:, 0:PT, :], d["x_prompt"].rearrange("(t p) n -> p t n", p=P)).then_inc(s_x, 16)
                act.dma_start(n.x[0:TS, PT, :], d["x_sample"]).then_inc(s_x, 16)
                act.wait_ge(s_c, 16)
                act.activation(cs[:], cT[:], ACT.Silu).then_inc(s_silu, 1)
                act.wait_ge(s_x, 32)
                for i in range(NCH):
                    r = tile_rows(i)
                    act.activation(junk[0:r], n.x[0:r, i, :], ACT.Square, accum_out=n.ss[0:r, i:i + 1]).then_inc(s_sq, 1)
                    act.wait_ge(s_sq, i + 1)
                act.wait_ge(s_ms, 2)
                act.activation(rt[:, 0:PT], ms[:, 0:PT], ACT.Sqrt)
                act.activation(rt[0:TS, PT:NCH], ms[0:TS, PT:NCH], ACT.Sqrt).then_inc(s_rt, 1)

            @block.tensor
            def _(pe):
                pe.wait_ge(s_silu, 1)
                for w in range(NCK):
                    pe.wait_ge(ready[w % NR], 16 * (w // NR + 1))
                    if w >= 2:
                        pe.wait_ge(s_add, w - 1)
                    for c in range(KD):
                        mm = pe.matmul(ps[0:NC, w % 2, :], cs[:, c, :], wring[:, w % NR, c, :],
                                       start=c == 0, stop=c == KD - 1)
                    mm.then_inc(s_mm, 1)
                pe.wait_ge(s_add, NCK)
                pe.wait_ge(s_const, 96)
                for a in range(2):
                    for c in range(KD):
                        mm = pe.transpose(ps[:, 2 + a, c * NC:(c + 1) * NC], mod[:, a, c * P:(c + 1) * P],
                                          k.ident[0:NC, 0:NC])
                mm.then_inc(s_tr, 1)

            @block.vector
            def _(dve):
                chain = Chain(dve, s_chain)

                def mean_squares():
                    dve.wait_ge(s_sq, NCH)
                    dve.tensor_scalar(ms[:, 0:PT], n.ss[:, 0:PT], 1.0 / D, EPS, ALU.mult, ALU.add).then_inc(s_ms, 1)
                    dve.tensor_scalar(ms[0:TS, PT:NCH], n.ss[0:TS, PT:NCH], 1.0 / D, EPS, ALU.mult,
                                      ALU.add).then_inc(s_ms, 1)

                def normalise():
                    dve.wait_ge(s_rt, 1)
                    dve.reciprocal(n.ss[:, 0:PT], rt[:, 0:PT])
                    chain.step(dve.reciprocal(n.ss[0:TS, PT:NCH], rt[0:TS, PT:NCH]))
                    for i in range(NCH):
                        r = tile_rows(i)
                        ins = dve.tensor_scalar(n.x[0:r, i, :], n.x[0:r, i, :], n.ss[0:r, i:i + 1], None, ALU.mult)
                    chain.step(ins)

                dve.wait_ge(s_b, 64)
                for w in range(NCK):
                    dve.wait_ge(s_mm, w + 1)
                    a, o = w // 2, (w % 2) * CHUNK
                    dve.tensor_tensor(mod[:, a, o:o + CHUNK], ps[0:NC, w % 2, :], bias[:, a, o:o + CHUNK],
                                      ALU.add).then_inc(s_add, 1)
                    if w == NORM_AT:
                        mean_squares()
                    if w == NORM_AT + 1:
                        normalise()
                dve.wait_ge(s_add, NCK)
                dve.tensor_tensor(mod[:, 2], mod[:, 2], grow[:, 0], ALU.mult).then_inc(s_rows, 1)
                dve.scalar_tensor_tensor(mod[:, 4], mod[:, 4], 1.0, grow[:, 1], ALU.add, ALU.mult).then_inc(s_rows, 1)
                dve.tensor_tensor(mod[:, 5], mod[:, 5], grow[:, 2], ALU.mult).then_inc(s_rows, 1)
                dve.wait_ge(s_tr, 1)
                dve.wait_ge(s_const, 96)
                for c in range(KD):
                    dve.tensor_copy(k.shift1[:, c, :], ps[:, 2, c * NC:(c + 1) * NC])
                    ins = dve.tensor_scalar(k.scale1[:, c, :], ps[:, 3, c * NC:(c + 1) * NC], 1.0, gcol[:, c:c + 1],
                                            ALU.add, ALU.mult)
                chain.step(ins)


def normalised_input(nc, k, d, n):
    x = n.x
    s_tr, s_ev, s_chain = (k.sem("ni_" + name) for name in ("tr", "ev", "chain"))
    ps = k.ps
    with nc.Block() as block:
        @block.scalar
        def _(act):
            for c in range(KD):
                act.wait_ge(s_tr, c + 1)
                act.activation(k.hT[:, c, 0:SEQ], ps[:, c % 4, :], ACT.Identity, scale=k.scale1[:, c, 0:1],
                               bias=k.shift1[:, c, 0:1]).then_inc(s_ev, 1)

        @block.tensor
        def _(pe):
            for c in range(KD):
                if c >= 4:
                    pe.wait_ge(s_ev, c - 3)
                for i in range(PT):
                    pe.transpose(ps[:, c % 4, i * P:(i + 1) * P], x[:, i, c * P:(c + 1) * P], k.ident[:])
                pe.transpose(ps[:, 4, c * TS:(c + 1) * TS], x[0:TS, PT, c * P:(c + 1) * P],
                             k.ident[0:TS, 0:TS]).then_inc(s_tr, 1)

        @block.vector
        def _(dve):
            chain = Chain(dve, s_chain)
            dve.wait_ge(s_tr, KD)
            for c in range(KD):
                out = k.hT[:, c, SEQ:T].rearrange("p (s l) -> p s l", s=NS)
                src = ps[:, 4, c * TS:(c + 1) * TS].rearrange("p (s l) -> p s l", s=NS)
                ins = dve.tensor_tensor(out, src, broadcast_mid(k.scale1[:, c, 1:NC], LS, 2), ALU.mult)
            chain.step(ins)
            for c in range(KD):
                out = k.hT[:, c, SEQ:T].rearrange("p (s l) -> p s l", s=NS)
                ins = dve.tensor_tensor(out, out, broadcast_mid(k.shift1[:, c, 1:NC], LS, 2), ALU.add)
            chain.step(ins)


def weight_ring(nc, k, name, ctx, slots):
    ring = Shared()
    ring.w = ctx.enter_context(nc.sbuf_tensor(name + "_ring", [P, slots, KD, CHUNK], F32))
    ring.ready = [k.sem(f"{name}_w_ready{r}") for r in range(slots)]
    ring.slots, ring.loaded = slots, 0
    return ring


def project(nc, k, name, rhsT, jobs, early=None):
    units = []
    for n, (kind, _, _) in enumerate(jobs):
        units += [(n, j) for j in range(CHUNK // P if kind == "feature" else NCH)]
    last_unit = {}
    for u, (n, _) in enumerate(units):
        last_unit[n] = u
    with ExitStack() as ctx:
        held = early or weight_ring(nc, k, name, ctx, NR)
        wring, ready, slots = held.w, held.ready, held.slots
        s_mm, s_ev = k.sem(name + "_mm"), k.sem(name + "_taken")
        ps = k.ps
        with nc.Block() as block:
            @block.gpsimd
            def _(pool):
                for u in range(len(units)):
                    if k.rolls:
                        pool.wait_ge(s_mm, u + 1)
                        dst, src = k.rolls.pop()
                        pool.dma_start(dst, src).then_inc(k.s_roll, 16)

            @block.sync
            def _(sp):
                for n in range(held.loaded, len(jobs)):
                    if n >= slots:
                        sp.wait_ge(s_mm, last_unit[n - slots] + 1)
                    sp.dma_start(wring[:, n % slots], jobs[n][1]).then_inc(ready[n % slots], 16)

            @block.tensor
            def _(pe):
                for u, (n, j) in enumerate(units):
                    if j == 0:
                        pe.wait_ge(ready[n % slots], 16 * (n // slots + 1))
                    if u >= 2:
                        pe.wait_ge(s_ev, u - 1)
                    w = wring[:, n % slots]
                    for c in range(KD):
                        on = dict(start=c == 0, stop=c == KD - 1)
                        if jobs[n][0] == "feature":
                            wc = w[:, c, j * P:(j + 1) * P]
                            pe.matmul(ps[:, u % 2, 0:TH], wc, rhsT[:, c, 0:TH], **on)
                            mm = pe.matmul(ps[:, 2 + u % 2, 0:TH], wc, rhsT[:, c, TH:T], **on)
                        else:
                            r = tile_rows(j)
                            mm = pe.matmul(ps[0:r, u % 2, :], rhsT[:, c, tile_cols(j)], w[:, c, :], **on)
                    mm.then_inc(s_mm, 1)

            @block.scalar
            def _(act):
                for u, (n, j) in enumerate(units):
                    act.wait_ge(s_mm, u + 1)
                    if jobs[n][0] == "feature":
                        ins = jobs[n][2](act, j, (ps[:, u % 2, 0:TH], ps[:, 2 + u % 2, 0:TH]))
                    else:
                        r = tile_rows(j)
                        ins = jobs[n][2](act, j, r, ps[0:r, u % 2, :])
                    ins.then_inc(s_ev, 1)


def attention_projections(nc, k, d, a):
    jobs = []
    for n in range(2 * G):
        def take(act, j, halves, n=n):
            act.activation(a.qk[:, H * n + j, 0:TH], halves[0], ACT.Copy)
            act.activation(a.qk[:, H * n + j, TH:SEQ], halves[1][:, 0:SEQ - TH], ACT.Copy)
            return act.activation(k.qkS[:, H * n + j, :], halves[1][:, SEQ - TH:], ACT.Copy)
        jobs.append(("feature", d["w_attn_qk"][n], take))
    for g in range(G):
        def take(act, j, r, res, g=g):
            return act.activation(a.v[:, j, g, :] if j < PT else k.vS[:, g, :], res, ACT.Copy)
        jobs.append(("token", d["w_attn_v"][g], take))
    project(nc, k, "ap", k.hT, jobs)


def prompt_attention(nc, k, d, a):
    steps = [(i, h) for i in range(PT) for h in range(H)]
    N = len(steps)
    with ExitStack() as ctx:
        sb = lambda n, s, dt=F32: ctx.enter_context(nc.sbuf_tensor(n, s, dt))
        masks = sb("pa_masks", [P, MASK_AT[PT]])
        prob = sb("pa_prob", [P, 2, NKMAX])
        probT = sb("pa_probT", [P, 2, NKMAX])
        mx = sb("pa_mx", [P, N, 4])
        nb = sb("pa_nb", [P, N])
        den = sb("pa_den", [P, N])
        rden = sb("pa_rden", [P, N])
        s_m, s_s, s_max, s_exp, s_norm, s_t, s_te, s_pv, s_o, s_chain, s_kv = (
            k.sem("pa_" + n) for n in ("masks", "scores", "max", "exp", "norm", "turned", "turned_taken", "pv",
                                       "out", "chain", "kv"))
        ps = k.ps
        flat = ps[:, 3:6, :].rearrange("p b n -> p (b n)")
        with nc.Block() as block:
            @block.sync
            def _(sp):
                sp.dma_start(masks[:], d["c_masks"]).then_inc(s_m, 16)
                for g in range(G):
                    sp.dma_start(d["kT_p"][g], a.qk[:, (2 * g + 1) * H:(2 * g + 2) * H, :]).then_inc(s_kv, 16)
                    sp.dma_start(d["v_p"][g], a.v[:, :, g, :]).then_inc(s_kv, 16)
                sp.wait_ge(s_kv, 16 * 2 * G)

            @block.tensor
            def _(pe):
                def scores(s):
                    i, h = steps[s]
                    if s >= 1:
                        pe.wait_ge(s_max, s)
                    for g, first, n, _ in key_cols(i):
                        mm = pe.matmul(ps[:, g, 0:n], a.qk[:, 2 * g * H + h, i * P:(i + 1) * P],
                                       a.qk[:, (2 * g + 1) * H + h, first:first + n], start=True, stop=True)
                    mm.then_inc(s_s, 1)

                scores(0)
                for s, (i, h) in enumerate(steps):
                    if s + 1 < N:
                        scores(s + 1)
                    pe.wait_ge(s_norm, s + 1)
                    if s >= 1:
                        pe.wait_ge(s_te, s)
                    nk = sum(n for _, _, n, _ in key_cols(i)) // P
                    for b in range(nk):
                        mm = pe.transpose(flat[:, b * P:(b + 1) * P], prob[:, s % 2, b * P:(b + 1) * P], k.ident[:])
                    mm.then_inc(s_t, 1)
                    pe.wait_ge(s_te, s + 1)
                    if s >= 2:
                        pe.wait_ge(s_o, s - 1)
                    b = 0
                    for g, first, n, _ in key_cols(i):
                        for t in range(first // P, (first + n) // P):
                            mm = pe.matmul(ps[:, 6 + s % 2, 0:P], a.v[:, t, g, h * P:(h + 1) * P],
                                           probT[:, s % 2, b * P:(b + 1) * P], start=b == 0, stop=b == nk - 1)
                            b += 1
                    mm.then_inc(s_pv, 1)

            @block.vector
            def _(dve):
                chain = Chain(dve, s_chain)
                dve.wait_ge(s_m, 16)
                for s, (i, h) in enumerate(steps):
                    dve.wait_ge(s_s, s + 1)
                    if s >= 2:
                        dve.wait_ge(s_t, s - 1)
                    for g, first, n, at in key_cols(i):
                        ins = dve.tensor_tensor_reduce(prob[:, s % 2, at:at + n], ps[:, g, 0:n],
                                                       masks[:, MASK_AT[i] + at:MASK_AT[i] + at + n], 1.0, 2 * NEG,
                                                       ALU.add, ALU.max, mx[:, s, g:g + 1])
                    chain.step(ins)
                    chain.step(dve.tensor_reduce(mx[:, s, 3:4], mx[:, s, 0:G], AX, ALU.max))
                    dve.tensor_scalar(nb[:, s:s + 1], mx[:, s, 3:4], -SCALE, None, ALU.mult).then_inc(s_max, 1)
                    dve.wait_ge(s_exp, s + 1)
                    chain.step(dve.reciprocal(rden[:, s:s + 1], den[:, s:s + 1]))
                    nk = sum(n for _, _, n, _ in key_cols(i))
                    dve.tensor_scalar(prob[:, s % 2, 0:nk], prob[:, s % 2, 0:nk], rden[:, s:s + 1], None,
                                      ALU.mult).then_inc(s_norm, 1)

            @block.scalar
            def _(act):
                def turned(s):
                    i, h = steps[s]
                    nk = sum(n for _, _, n, _ in key_cols(i))
                    act.wait_ge(s_t, s + 1)
                    if s >= 2:
                        act.wait_ge(s_pv, s - 1)
                    for b in range(0, nk, 512):
                        m = min(512, nk - b)
                        ins = act.activation(probT[:, s % 2, b:b + m], flat[:, b:b + m], ACT.Copy)
                    ins.then_inc(s_te, 1)
                    act.wait_ge(s_pv, s + 1)
                    act.activation(k.oaT[:, h, i * P:(i + 1) * P], ps[:, 6 + s % 2, 0:P], ACT.Copy).then_inc(s_o, 1)

                for s, (i, h) in enumerate(steps):
                    nk = sum(n for _, _, n, _ in key_cols(i))
                    act.wait_ge(s_max, s + 1)
                    act.activation(prob[:, s % 2, 0:nk], prob[:, s % 2, 0:nk], ACT.Exp, bias=nb[:, s:s + 1],
                                   scale=SCALE, accum_out=den[:, s:s + 1]).then_inc(s_exp, 1)
                    if s >= 1:
                        turned(s - 1)
                turned(N - 1)


def mlstm_projections(nc, k, d, m):
    def take_raw(n):
        def take(act, j, halves):
            b = H * n + j
            act.activation(m.raw[:, b, CW - 1:CW - 1 + TH], halves[0], ACT.Copy)
            act.activation(m.raw[:, b, CW - 1 + TH:CW - 1 + SEQ], halves[1][:, 0:SEQ - TH], ACT.Copy)
            sample = halves[1][:, SEQ - TH:]
            out = m.rawS[:, b].rearrange("p (s l) -> p s l", s=NS)[:, :, CW - 1:CW - 1 + LS]
            return act.activation(out, sample.rearrange("p (s l) -> p s l", s=NS), ACT.Copy)
        return take

    def take_v(act, j, r, res):
        return act.activation(m.v[0:r, j, :], res, ACT.Copy)

    def take_o(act, j, r, res):
        return act.activation(m.o[0:r, j, :], res, ACT.Sigmoid)

    project(nc, k, "mp", k.hT, [("feature", d["w_qk"][0], take_raw(0)), ("feature", d["w_qk"][1], take_raw(1)),
                                ("token", d["w_mv"], take_v), ("token", d["w_mo"], take_o)])


class MergeGates:

    UNITS = 2 * KD
    AHEAD = 4
    BANK = 6

    def __init__(self, nc, k, d, ctx):
        self.k, self.d = k, d
        self.gate = ctx.enter_context(nc.sbuf_tensor("gate", [P, self.UNITS, T], F32))
        self.ready = [k.sem(f"gate_w_ready{r}") for r in range(self.AHEAD)]
        self.s_mm, self.s_taken = k.sem("gate_mm"), k.sem("gate_taken")

    def allocate_ring(self, nc, ctx):
        self.ring = ctx.enter_context(nc.sbuf_tensor("gate_ring", [P, self.AHEAD, KD, P], F32))

    def load(self, sp, units):
        for u in units:
            if u >= self.AHEAD:
                sp.wait_ge(self.s_mm, 2 * (u - self.AHEAD + 1))
            sp.dma_start(self.ring[:, u % self.AHEAD], self.d["w_merge"][u]).then_inc(self.ready[u % self.AHEAD], 16)

    def product(self, pe, halves):
        for n in halves:
            u, half = divmod(n, 2)
            if half == 0:
                pe.wait_ge(self.ready[u % self.AHEAD], 16 * (u // self.AHEAD + 1))
            if n >= 2:
                pe.wait_ge(self.s_taken, n - 1)
            for c in range(KD):
                mm = pe.matmul(self.k.ps[:, self.BANK + half, 0:TH], self.ring[:, u % self.AHEAD, c, :],
                               self.k.hT[:, c, half * TH:(half + 1) * TH], start=c == 0, stop=c == KD - 1)
            mm.then_inc(self.s_mm, 1)

    def take(self, act, halves):
        for n in halves:
            u, half = divmod(n, 2)
            act.wait_ge(self.s_mm, n + 1)
            act.activation(self.gate[:, u, half * TH:(half + 1) * TH], self.k.ps[:, self.BANK + half, 0:TH],
                           ACT.Copy).then_inc(self.s_taken, 1)

    def roll(self, pool, units):
        for u in units:
            if self.k.rolls:
                pool.wait_ge(self.s_mm, 2 * (u + 1))
                dst, src = self.k.rolls.pop()
                pool.dma_start(dst, src).then_inc(self.k.s_roll, 16)


CG_TAKES = (3, 2, 2, 2, 2, 2, 1, 1, 1)
CG_HALVES = sum(CG_TAKES)
ML_HALVES = ((2, 2),) + ((1, 2),) * 4


A_, W_, E_, X_ = range(4)


def conv_and_gates(nc, k, d, m, gates):
    RAWS = NS * (CW - 1 + LS)
    with ExitStack() as ctx:
        sb = lambda n, s, dt=F32: ctx.enter_context(nc.sbuf_tensor(n, s, dt))
        state = sb("cg_state", [P, 2 * H, NS, CW - 1])
        cw = sb("cg_w", [P, 2 * H, CW + 1])
        acc = sb("cg_acc", [P, 2 * H, T])
        newp = sb("cg_newp", [P, 2 * H, CW - 1])
        news = sb("cg_news", [P, 2 * H, NS, CW - 1])
        wg = sb("cg_wg", [P, KD, 2 * H])
        gb = sb("cg_gb", [H, 2])
        m0 = sb("cg_m0", [H, NS])
        carry = sb("cg_carry", [H, T])
        restart = sb("cg_restart", [H, T])
        ig = sb("cg_ig", [H, T])
        fg = sb("cg_fg", [H, T])
        lf = sb("cg_lf", [H, T])
        e = sb("cg_e", [H, T])
        bb = sb("cg_b", [H, T])
        mt = sb("cg_mt", [H, T])
        mprev = sb("cg_mprev", [H, PT + NS])
        mlast = sb("cg_mlast", [H, PT + NS])
        mnew = sb("cg_mnew", [H, 1 + NS])
        s_in, s_st, s_gm, s_gt, s_lf, s_f, s_cv, s_silu, s_rows, s_exp, s_tr, s_chain, s_out, s_new, s_mn, s_sc = (
            k.sem("cg_" + n) for n in ("in", "state", "gate_mm", "gate_taken", "logf", "f_abs", "conv", "silu", "rows",
                                       "exp", "turned", "chain", "out", "new", "mnew", "kscale"))
        s_one = k.sem("cg_act")
        ps = k.ps

        def rows(t):
            return t[:, 0:SEQ].rearrange("h (c t) -> h c t", c=PT), t[:, SEQ:T].rearrange("h (s l) -> h s l", s=NS)

        with nc.Block() as block:
            @block.sync
            def _(sp):
                for dst, src in ((state[:], "stateT"), (cw[:], "conv_w"), (wg[:], "w_gates"), (gb[:], "b_gates"),
                                 (m0[:], "m0"), (carry[:], "c_carry"), (restart[:], "c_restart")):
                    sp.dma_start(dst, d[src]).then_inc(s_in, 16)
                gates.load(sp, range(CG_HALVES // 2))
                sp.wait_ge(s_new, 2)
                sp.dma_start(d["conv_p"], newp[:]).then_inc(s_out, 16)
                sp.dma_start(d["conv_s"], news[:]).then_inc(s_out, 16)
                sp.wait_ge(s_mn, 2)
                sp.dma_start(d["m_new"], mnew[:]).then_inc(s_out, 16)
                gates.load(sp, range(CG_HALVES // 2, CG_HALVES // 2 + gates.AHEAD))
                sp.wait_ge(s_out, 48)

            @block.gpsimd
            def _(pool):
                pool.memset(m.ones[:], 1.0)
                gates.roll(pool, range(CG_HALVES // 2))
                pool.wait_ge(s_silu, 2 * H)
                for b in range(H, 2 * H):
                    ins = pool.tensor_scalar(m.qk[:, b, :], m.qk[:, b, :], SCALE, None, ALU.mult)
                ins.then_inc(s_sc, 1)
                pool.wait_ge(s_sc, 1)

            @block.tensor
            def _(pe):
                pe.wait_ge(s_in, 7 * 16)
                for gate in range(2):
                    for part, cols in ((0, slice(0, SEQ)), (1, slice(SEQ, T))):
                        n = cols.stop - cols.start
                        for c in range(KD):
                            mm = pe.matmul(ps[0:H, 2 * gate + part, 0:n], wg[:, c, gate * H:(gate + 1) * H],
                                           k.hT[:, c, cols], start=c == 0, stop=c == KD - 1)
                mm.then_inc(s_gm, 1)
                gates.product(pe, range(CG_HALVES))
                pe.wait_ge(s_exp, 1)
                for c in range(NCH):
                    r = tile_rows(c)
                    for kind in range(4):
                        o = (c * 4 + kind) * H
                        mm = pe.matmul(ps[0:r, 4, o:o + H], m.rows[:, kind, tile_cols(c)], k.ident[0:H, 0:H],
                                       start=True, stop=True)
                for h in range(H):
                    mm = pe.matmul(ps[:, 5, h * (PT + NS):(h + 1) * (PT + NS)], k.sel[:, h * P:(h + 1) * P],
                                   m.decay[:], start=True, stop=True)
                mm.then_inc(s_tr, 1)

            @block.scalar
            def _(act):
                chain = Chain(act, s_one)
                act.wait_ge(s_gm, 1)
                for gate, dst in ((0, ig), (1, fg)):
                    act.activation(dst[:, 0:SEQ], ps[0:H, 2 * gate, :], ACT.Identity, bias=gb[:, gate:gate + 1])
                    ins = act.activation(dst[:, SEQ:T], ps[0:H, 2 * gate + 1, 0:TS], ACT.Identity,
                                         bias=gb[:, gate:gate + 1])
                chain.step(ins)
                chain.step(act.activation(e[:], fg[:], ACT.Abs))
                chain.step(act.activation(e[:], e[:], ACT.Exp, scale=-1.0))
                act.activation(e[:], e[:], ACT.Ln, bias=1.0).then_inc(s_f, 1)
                gates.take(act, range(CG_TAKES[0]))
                taken = CG_TAKES[0]
                act.wait_ge(s_rows, 1)
                for kind in (A_, W_, E_, X_):
                    if kind != A_:
                        ins = act.activation(m.rows[:, kind, :], m.rows[:, kind, :], ACT.Exp)
                act.activation(m.decay[:], m.decay[:], ACT.Exp).then_inc(s_exp, 1)
                for b in range(2 * H):
                    act.wait_ge(s_cv, b + 1)
                    act.activation(m.qk[:, b, :], acc[:, b, :], ACT.Silu).then_inc(s_silu, 1)
                    gates.take(act, range(taken, taken + CG_TAKES[1 + b]))
                    taken += CG_TAKES[1 + b]

            @block.vector
            def _(dve):
                chain = Chain(dve, s_chain)
                dve.wait_ge(s_in, 7 * 16)
                dve.memset(m.raw[:, :, 0:CW - 1], 0.0)
                head = m.rawS[:].rearrange("p b (s l) -> p b s l", s=NS)
                for b in range(2 * H):
                    ins = dve.tensor_copy(head[:, b, :, 0:CW - 1], state[:, b])
                chain.step(ins)
                dve.tensor_copy(newp[:], m.raw[:, :, SEQ:SEQ + CW - 1]).then_inc(s_new, 1)
                for b in range(2 * H):
                    ins = dve.tensor_copy(news[:, b], head[:, b, :, LS:LS + CW - 1])
                ins.then_inc(s_new, 1)
                dve.wait_ge(s_f, 1)
                dve.memset(mprev[:, 0:1], 0.0)
                chain.step(dve.tensor_scalar(lf[:], fg[:], 0.0, None, ALU.min))
                chain.step(dve.tensor_tensor(lf[:], lf[:], e[:], ALU.subtract))
                chain.step(dve.tensor_tensor_scan(bb[:], carry[:], lf[:], 0.0, ALU.mult, ALU.add))
                first = lambda t: t[:, SEQ:T].rearrange("h (s l) -> h s l", s=NS)[:, :, 0]
                dve.tensor_copy(e[:], ig[:])
                chain.step(dve.tensor_tensor(mprev[:, PT:], first(lf), m0[:], ALU.add))
                chain.step(dve.tensor_tensor(first(e), first(e), mprev[:, PT:], ALU.max))
                chain.step(dve.tensor_tensor(fg[:], lf[:], restart[:], ALU.add))
                chain.step(dve.tensor_tensor_scan(mt[:], fg[:], e[:], 0.0, ALU.add, ALU.max))
                mtp, mts = rows(mt)
                bp, bs = rows(bb)
                dve.tensor_copy(mprev[:, 1:PT], mtp[:, 0:PT - 1, P - 1])
                dve.tensor_copy(mprev[:, PT:], m0[:])
                dve.tensor_copy(mnew[:, 0:1], mtp[:, PT - 1, P - 1:P])
                dve.tensor_copy(mnew[:, 1:], mts[:, :, LS - 1]).then_inc(s_mn, 2)
                chain.step(dve.tensor_tensor(m.M[:], mt[:], bb[:], ALU.subtract))
                Mp, Ms = rows(m.M)
                dve.tensor_copy(mlast[:, 0:PT], Mp[:, :, P - 1])
                dve.tensor_copy(mlast[:, PT:], Ms[:, :, LS - 1])
                chain.step(dve.tensor_tensor(m.rows[:, A_, :], ig[:], bb[:], ALU.subtract))
                chain.step(dve.tensor_scalar(m.rows[:, E_, :], mt[:], -1.0, None, ALU.mult))
                for kind, sign in ((W_, 0), (X_, 1)):
                    outp, outs = rows(m.rows[:, kind, :])
                    if kind == W_:
                        dve.tensor_tensor(outp, broadcast_mid(mprev[:, 0:PT], P, 2), Mp, ALU.subtract)
                        dve.tensor_tensor(outs, broadcast_mid(mprev[:, PT:], LS, 2), Ms, ALU.subtract)
                    else:
                        ap_, as_ = rows(m.rows[:, A_, :])
                        dve.tensor_tensor(outp, ap_, broadcast_mid(mlast[:, 0:PT], P, 2), ALU.subtract)
                        dve.tensor_tensor(outs, as_, broadcast_mid(mlast[:, PT:], LS, 2), ALU.subtract)
                dve.tensor_tensor(m.decay[:], mprev[:], mlast[:], ALU.subtract).then_inc(s_rows, 1)
                for b in range(2 * H):
                    raw = m.raw[:, b, :]
                    rs = m.rawS[:, b].rearrange("p (s l) -> p s l", s=NS)
                    op, os_ = acc[:, b, 0:SEQ], acc[:, b, SEQ:T].rearrange("p (s l) -> p s l", s=NS)
                    dve.tensor_scalar(op, raw[:, 0:SEQ], cw[:, b, 0:1], cw[:, b, CW:CW + 1], ALU.mult, ALU.add)
                    chain.step(dve.tensor_scalar(os_, rs[:, :, 0:LS], cw[:, b, 0:1], cw[:, b, CW:CW + 1],
                                                 ALU.mult, ALU.add))
                    for j in range(1, CW):
                        dve.scalar_tensor_tensor(op, raw[:, j:j + SEQ], cw[:, b, j:j + 1], op, ALU.mult, ALU.add)
                        ins = dve.scalar_tensor_tensor(os_, rs[:, :, j:j + LS], cw[:, b, j:j + 1], os_,
                                                       ALU.mult, ALU.add)
                        if j < CW - 1:
                            chain.step(ins)
                    ins.then_inc(s_cv, 1)
                dve.wait_ge(s_tr, 1)
                for c in range(NCH):
                    r = tile_rows(c)
                    dve.tensor_copy(m.cols[0:r, c], ps[0:r, 4, c * 16:(c + 1) * 16].rearrange("p (k h) -> p k h", k=4))
                chain.step(dve.tensor_copy(m.dcols[:], ps[:, 5, 0:H * (PT + NS)].rearrange("p (h n) -> p h n", h=H)))


def mlstm(nc, k, d, m, gates):
    LAST = NCH - 1
    with ExitStack() as ctx:
        sb = lambda n, s, dt=F32: ctx.enter_context(nc.sbuf_tensor(n, s, dt))
        C = sb("ml_C", [P, H, P])
        n_ = sb("ml_n", [P, H])
        C0 = sb("ml_C0", [P, NS, H, P])
        n0 = sb("ml_n0", [P, NS, H])
        tri = sb("ml_tri", [P, P])
        stri = sb("ml_stri", [P, TS])
        mhg = sb("ml_mhg", [P, H])
        w = sb("ml_w", [P, H, P])
        sT = sb("ml_sT", [P, H, P])
        kw = sb("ml_kw", [P, H, P])
        ks = sb("ml_ks", [P, 2, H, P])
        iw = sb("ml_iw", [P, H, P])
        hn = sb("ml_hn", [P, H, P])
        sq = sb("ml_sq", [P, H, P])
        dn = sb("ml_dn", [P, H])
        rd = sb("ml_rd", [P, H])
        ss = sb("ml_ss", [P, H])
        ms = sb("ml_ms", [P, H])
        rt = sb("ml_rt", [P, H])
        qm = sb("ml_qm", [P, H, NS * (TS + LS)])
        s_in, s_pre, s_e, s_w, s_s, s_mid, s_iw, s_ms, s_rt, s_hn, s_tr, s_tt, s_c, s_ks, s_su, s_sc, s_z, s_qm, s_out, s_chain = (
            k.sem("ml_" + n) for n in ("in", "pre", "expo", "w", "s", "mid", "inter", "ms", "root", "h", "turned",
                                       "turned_taken", "state", "kmask", "seq_update", "seq_state", "zero", "qmask",
                                       "out", "chain"))
        ps = k.ps
        by_head = lambda bank, r: ps[0:r, bank, :].rearrange("p (h t) -> p h t", h=H)
        with nc.Block() as block:
            @block.sync
            def _(sp):
                sp.dma_start(tri[:], d["c_tri"]).then_inc(s_in, 16)
                sp.dma_start(stri[:], d["c_stri"]).then_inc(s_in, 16)
                sp.dma_start(mhg[:], d["mh_norm_g"]).then_inc(s_in, 16)
                sp.dma_start(C0[:], d["C0"]).then_inc(s_in, 16)
                sp.dma_start(n0[:], d["n0"]).then_inc(s_in, 16)
                gates.load(sp, range(CG_HALVES // 2 + gates.AHEAD, gates.UNITS))
                sp.wait_ge(s_c, PT)
                sp.dma_start(d["C_p"], C[:]).then_inc(s_out, 16)
                sp.dma_start(d["n_p"], n_[:]).then_inc(s_out, 16)
                sp.wait_ge(s_sc, NS)
                sp.dma_start(d["C_s"], C0[:]).then_inc(s_out, 16)
                sp.dma_start(d["n_s"], n0[:]).then_inc(s_out, 16)
                sp.wait_ge(s_out, 64)

            @block.gpsimd
            def _(pool):
                pool.memset(C[:], 0.0).then_inc(s_z, 1)
                pool.memset(n_[:], 0.0).then_inc(s_z, 1)
                pool.memset(qm[:], 0.0).then_inc(s_z, 1)
                pool.wait_ge(s_z, 3)
                for h in range(H):
                    out = qm[:, h, :].rearrange("p (s r) -> p s r", r=TS + LS)[:, :, 0:LS]
                    ins = pool.tensor_copy(out, m.qk[:, h, SEQ:T].rearrange("p (s l) -> p s l", s=NS))
                ins.then_inc(s_qm, 1)
                gates.roll(pool, range(CG_HALVES // 2, gates.UNITS))

            @block.tensor
            def _(pe):
                done = CG_HALVES
                for c in range(NCH):
                    r, cols = tile_rows(c), tile_cols(c)
                    if c >= 1:
                        pe.wait_ge(s_c, c)
                        pe.wait_ge(s_iw, c)
                        pe.wait_ge(s_hn, c)
                    for h in range(H):
                        o = h * P
                        pe.transpose(ps[0:r, 0, o:o + P], m.qk[:, H + h, cols], k.ident[:])
                        pe.matmul(ps[0:r, 1, o:o + r], k.sel[:, o:o + r], m.M[:, cols], start=True, stop=True)
                        mm = pe.matmul(ps[0:r, 2, o:o + r], m.qk[:, H + h, cols], m.qk[:, h, cols],
                                       start=True, stop=True)
                    mm.then_inc(s_pre, 1)
                    gates.product(pe, range(done, done + ML_HALVES[c][0]))
                    done += ML_HALVES[c][0]
                    pe.wait_ge(s_s, c + 1)
                    if c == 0:
                        pe.wait_ge(s_z, 3)
                    if c == LAST:
                        pe.wait_ge(s_qm, 1)
                        pe.wait_ge(s_in, 80)
                    for h in range(H):
                        o = h * P
                        vh = m.v[0:r, c, o:o + P]
                        pe.matmul(ps[0:r, 1, o:o + P], sT[0:r, h, 0:r], vh, start=True, stop=True)
                        pe.matmul(ps[0:r, 0, h:h + 1], sT[0:r, h, 0:r], m.ones[0:r, 0:1], start=True, stop=True)
                        if c < LAST:
                            pe.matmul(ps[0:r, 2, o:o + P], m.qk[:, h, cols], C[:, h, :], start=True, stop=True)
                            pe.matmul(ps[0:r, 0, H + h:H + h + 1], m.qk[:, h, cols], n_[:, h:h + 1],
                                      start=True, stop=True)
                            pe.matmul(ps[:, 3, o:o + P], kw[0:r, h, :], vh, start=True, stop=True)
                            mm = pe.matmul(ps[:, 0, 2 * H + h:2 * H + h + 1], kw[0:r, h, :], m.ones[0:r, 0:1],
                                           start=True, stop=True)
                        else:
                            for s in range(NS):
                                on = dict(start=s == 0, stop=s == NS - 1)
                                q = qm[:, h, s * TS:(s + 1) * TS]
                                pe.matmul(ps[0:r, 2, o:o + P], q, C0[:, s, h, :], **on)
                            for s in range(NS):
                                on = dict(start=s == 0, stop=s == NS - 1)
                                q = qm[:, h, s * TS:(s + 1) * TS]
                                mm = pe.matmul(ps[0:r, 0, H + h:H + h + 1], q, n0[:, s, h:h + 1], **on)
                    mm.then_inc(s_mid, 1)
                    gates.product(pe, range(done, done + ML_HALVES[c][1]))
                    done += ML_HALVES[c][1]
                    pe.wait_ge(s_hn, c + 1)
                    if c >= 1:
                        pe.wait_ge(s_tt, c)
                    for h in range(H):
                        mm = pe.transpose(ps[:, 4, h * P:h * P + r], hn[0:r, h, :], k.ident[0:r, 0:r])
                    mm.then_inc(s_tr, 1)
                pe.wait_ge(gates.s_taken, 2 * gates.UNITS)
                for s in range(NS):
                    pe.wait_ge(s_ks, s + 1)
                    if s >= 2:
                        pe.wait_ge(s_sc, s - 1)
                    for h in range(H):
                        pe.matmul(ps[:, 5 + s % 2, h * P:(h + 1) * P], ks[0:TS, s % 2, h, :],
                                  m.v[0:TS, LAST, h * P:(h + 1) * P], start=True, stop=True)
                        mm = pe.matmul(ps[:, 3 if s % 2 else 7, h:h + 1], ks[0:TS, s % 2, h, :], m.ones[0:TS, 0:1],
                                       start=True, stop=True)
                    mm.then_inc(s_su, 1)

            @block.scalar
            def _(act):
                done = CG_HALVES
                for c in range(NCH):
                    r, cols = tile_rows(c), tile_cols(c)
                    before, after = ML_HALVES[c]
                    act.wait_ge(s_e, c + 1)
                    for h in range(H):
                        ins = act.activation(w[0:r, h, 0:r], w[0:r, h, 0:r], ACT.Exp, bias=m.cols[0:r, c, A_, h:h + 1])
                    ins.then_inc(s_w, 1)
                    gates.take(act, range(done, done + before))
                    act.wait_ge(s_mid, c + 1)
                    for h in range(H):
                        ins = act.activation(iw[0:r, h, :], by_head(2, r)[:, h, :], ACT.Copy,
                                             scale=m.cols[0:r, c, W_, h:h + 1])
                    ins.then_inc(s_iw, 1)
                    gates.take(act, range(done + before, done + before + after - 1))
                    act.wait_ge(s_ms, c + 1)
                    act.activation(rt[0:r], ms[0:r], ACT.Sqrt).then_inc(s_rt, 1)
                    done += before + after
                    gates.take(act, range(done - 1, done))
                    act.wait_ge(s_tr, c + 1)
                    act.wait_ge(s_in, 80)
                    for h in range(H):
                        ins = act.activation(k.hmT[:, h, cols], ps[:, 4, h * P:h * P + r], ACT.Copy,
                                             scale=mhg[:, h:h + 1])
                    ins.then_inc(s_tt, 1)

            @block.vector
            def _(dve):
                chain = Chain(dve, s_chain)
                dve.wait_ge(s_in, 80)
                for c in range(NCH):
                    r = tile_rows(c)
                    mask = tri[0:r, 0:r] if c < LAST else stri[0:r, 0:r]
                    dve.wait_ge(s_pre, c + 1)
                    dve.tensor_tensor(w[0:r, :, 0:r], broadcast_mid(mask, H, 1), by_head(1, r)[:, :, 0:r],
                                      ALU.subtract).then_inc(s_e, 1)
                    for h in range(H):
                        dve.tensor_scalar(kw[0:r, h, :], by_head(0, r)[:, h, :], m.cols[0:r, c, X_, h:h + 1], None,
                                          ALU.mult)
                    dve.wait_ge(s_w, c + 1)
                    dve.tensor_tensor(sT[0:r, :, 0:r], w[0:r, :, 0:r], by_head(2, r)[:, :, 0:r],
                                      ALU.mult).then_inc(s_s, 1)
                    dve.wait_ge(s_mid, c + 1)
                    chain.step(dve.tensor_tensor(dn[0:r], ps[0:r, 0, H:2 * H], m.cols[0:r, c, W_, :], ALU.mult))
                    chain.step(dve.tensor_tensor(dn[0:r], ps[0:r, 0, 0:H], dn[0:r], ALU.add))
                    chain.step(dve.scalar_tensor_tensor(dn[0:r], dn[0:r], -1.0, dn[0:r], ALU.mult, ALU.max))
                    chain.step(dve.tensor_tensor(dn[0:r], dn[0:r], m.cols[0:r, c, E_, :], ALU.max))
                    chain.step(dve.reciprocal(rd[0:r], dn[0:r]))
                    if c < LAST:
                        for h in range(H):
                            dc = m.dcols[:, h, c:c + 1]
                            dve.scalar_tensor_tensor(C[:, h, :], C[:, h, :], dc, ps[:, 3, h * P:(h + 1) * P],
                                                     ALU.mult, ALU.add)
                            ins = dve.scalar_tensor_tensor(n_[:, h:h + 1], n_[:, h:h + 1], dc,
                                                           ps[:, 0, 2 * H + h:2 * H + h + 1], ALU.mult, ALU.add)
                        ins.then_inc(s_c, 1)
                    dve.wait_ge(s_iw, c + 1)
                    chain.step(dve.tensor_tensor(hn[0:r], iw[0:r], by_head(1, r), ALU.add))
                    chain.step(dve.tensor_tensor(hn[0:r], hn[0:r],
                                                 m.o[0:r, c, :].rearrange("p (h t) -> p h t", h=H), ALU.mult))
                    chain.step(dve.tensor_tensor(hn[0:r], hn[0:r], broadcast_mid(rd[0:r], P, 2), ALU.mult))
                    chain.step(dve.tensor_tensor(sq[0:r], hn[0:r], hn[0:r], ALU.mult))
                    chain.step(dve.tensor_reduce(ss[0:r], sq[0:r], AX, ALU.add))
                    dve.tensor_scalar(ms[0:r], ss[0:r], 1.0 / P, EPS, ALU.mult, ALU.add).then_inc(s_ms, 1)
                    dve.wait_ge(s_rt, c + 1)
                    chain.step(dve.reciprocal(rd[0:r], rt[0:r]))
                    dve.tensor_tensor(hn[0:r], hn[0:r], broadcast_mid(rd[0:r], P, 2), ALU.mult).then_inc(s_hn, 1)
                    dve.wait_ge(s_tr, c + 1)
                for s in range(NS + 1):
                    if s < NS:
                        if s >= 2:
                            dve.wait_ge(s_su, s - 1)
                        dve.tensor_scalar(ks[0:TS, s % 2], kw[0:TS], k.block[:, s:s + 1], None,
                                          ALU.mult).then_inc(s_ks, 1)
                    if s >= 1:
                        q = s - 1
                        dve.wait_ge(s_su, q + 1)
                        for h in range(H):
                            dc = m.dcols[:, h, PT + q:PT + q + 1]
                            dve.scalar_tensor_tensor(C0[:, q, h, :], C0[:, q, h, :], dc,
                                                     ps[:, 5 + q % 2, h * P:(h + 1) * P], ALU.mult, ALU.add)
                            ins = dve.scalar_tensor_tensor(n0[:, q, h:h + 1], n0[:, q, h:h + 1], dc,
                                                           ps[:, 3 if q % 2 else 7, h:h + 1], ALU.mult, ALU.add)
                        ins.then_inc(s_sc, 1)


UNITS = ([(0, 0)] + [(1, r) for r in range(RES[1])], [(2, r) for r in range(RES[2])])
NZ = 3
SR = 4


def sample_attention(nc, k, d):
    GH = G * H
    ALLU = UNITS[0] + UNITS[1]
    NW = len(ALLU) * H
    jobs = [(v, s, part) for v in range(2) for s in range(NS) for part in range(2)]
    with ExitStack() as ctx:
        sb = lambda n, s, dt=F32: ctx.enter_context(nc.sbuf_tensor(n, s, dt))
        ring = sb("sa_ring", [P, SR, RES[2] * H * P])
        spread = sb("sa_spread", [P, NZ, (NW + 1) * TS])
        smask = sb("sa_mask", [TS, G, P + TS])
        sc = sb("sa_sc", [TS, H, G, P + TS])
        pN = sb("sa_pN", [TS, GH, TS])
        oN = sb("sa_oN", [TS, H, P])
        mx = sb("sa_mx", [TS, H])
        nb = sb("sa_nb", [TS, H])
        den = sb("sa_den", [TS, H])
        rden = sb("sa_rden", [TS, H])
        ready = [k.sem(f"sa_ready{r}") for r in range(SR)]
        s_m, s_used, s_spread, s_tr, s_nb, s_exp, s_norm, s_pt, s_pe, s_chain, s_new = (
            k.sem("sa_" + n) for n in ("mask", "used", "spread", "scores", "max", "exp", "norm", "turned", "taken",
                                       "chain", "new"))
        ps = k.ps

        def operand(n, s, w):
            o = (w + 1) * TS - (s + 1) * LS
            return spread[:, n % NZ, o:o + TS]

        def places(n, g):
            o = [u[0] for u in ALLU].index(g) * H * TS + TS - LS
            step = H * TS + 1
            v = spread[:, n % NZ, o:o + RES[g] * step].rearrange("p (r x) -> p r x", x=step)[:, :, 0:H * TS]
            return v.rearrange("p r (h y) -> p r h y", y=TS)[:, :, :, 0:LS - RES[g] + 1:RES[g]]

        with nc.Block() as block:
            @block.sync
            def _(sp):
                for n, (v, s, part) in enumerate(jobs):
                    if n == 1:
                        sp.dma_start(smask[:].rearrange("p g n -> p (g n)"), d["c_smask"]).then_inc(s_m, 16)
                    if n >= SR:
                        sp.wait_ge(s_used, n - SR + 1)
                    units = UNITS[part]
                    if v == 0:
                        dst = ring[:, n % SR, 0:len(units) * H * P]
                        src = d["kcacheA" if part == 0 else "kcacheB"][s]
                        sp.dma_start(dst, src).then_inc(ready[n % SR], 16)
                    else:
                        for g in sorted({g for g, _ in units}):
                            at = [u[0] for u in units].index(g)
                            dst = ring[:, n % SR, at * H * P:(at + RES[g]) * H * P].rearrange("p (r n) -> p r n", r=RES[g])
                            src = d[f"cache{g}"][s].rearrange("(j r two n) -> j r two n", r=DILATIONS[g], two=2,
                                                              n=H * P)[:, 0:RES[g], 1, :]
                            sp.dma_start(dst, src).then_inc(ready[n % SR], 16)
                for g in range(G):
                    sp.dma_start(d["kT_s"][g], k.qkS[:, (2 * g + 1) * H:(2 * g + 2) * H, :]).then_inc(s_new, 16)
                sp.dma_start(d["v_s"], k.vS[0:TS]).then_inc(s_new, 16)
                sp.wait_ge(s_new, 16 * (G + 1))

            def softmax_products(pe):
                for gh in range(GH):
                    g, h = divmod(gh, H)
                    mm = pe.matmul(ps[0:TS, 5 + gh // 8, (gh % 8) * TS:(gh % 8 + 1) * TS], k.qkS[:, 2 * g * H + h, :],
                                   k.qkS[:, (2 * g + 1) * H + h, :], start=True, stop=True)
                mm.then_inc(s_tr, 1)
                pe.wait_ge(s_norm, 1)
                for gh in range(GH):
                    g, h = divmod(gh, H)
                    pe.transpose(ps[:, gh // 8, (gh % 8) * TS:(gh % 8 + 1) * TS], sc[:, h, g, 0:P], k.ident[0:TS, 0:TS])
                    mm = pe.transpose(ps[0:TS, 2 + gh // 8, (gh % 8) * TS:(gh % 8 + 1) * TS], sc[:, h, g, P:],
                                      k.ident[0:TS, 0:TS])
                mm.then_inc(s_pt, 1)
                pe.wait_ge(s_pe, 1)
                for gh in range(GH):
                    g, h = divmod(gh, H)
                    pe.matmul(ps[0:TS, 4 + h, 0:P], pN[:, gh, :], k.vS[0:TS, g, h * P:(h + 1) * P],
                              start=g == 0, stop=False, skip_group_check=True)

            @block.tensor
            def _(pe):
                arrived = [0] * SR
                pe.wait_ge(s_spread, 1)
                for g in range(G):
                    pe.matmul(ps[0:TS, 2 + g, :], spread[:, 0, NW * TS:], k.hT[:, 0, 0:H * P], start=True, stop=False,
                              skip_group_check=True)
                for n, (v, s, part) in enumerate(jobs):
                    if n == NS * 2:
                        softmax_products(pe)
                    arrived[n % SR] += 16 * (2 if v and part == 0 else 1)
                    pe.wait_ge(s_spread, n // 2 + 1)
                    pe.wait_ge(ready[n % SR], arrived[n % SR])
                    for u, (g, r) in enumerate(UNITS[part]):
                        last = s == NS - 1 and r == RES[g] - 1 and (v == 0 or g == G - 1)
                        for h in range(H):
                            w = (u + part * len(UNITS[0])) * H + h
                            o = ps[0:TS, 4 + h, 0:P] if v else ps[0:TS, 2 + g, h * P:(h + 1) * P]
                            mm = pe.matmul(o, operand(n // 2, s, w), ring[:, n % SR, (u * H + h) * P:(u * H + h + 1) * P],
                                           start=False, stop=last, skip_group_check=True)
                    mm.then_inc(s_used, 1)
                pe.wait_ge(s_pe, 2)
                for h in range(H):
                    mm = pe.transpose(ps[:, 0, h * TS:(h + 1) * TS], oN[:, h, :], k.ident[0:TS, 0:TS])
                mm.then_inc(s_pt, 1)

            @block.scalar
            def _(act):
                act.wait_ge(s_nb, 1)
                for h in range(H):
                    v = sc[:, h].rearrange("p g n -> p (g n)")
                    ins = act.activation(v, v, ACT.Exp, bias=nb[:, h:h + 1], scale=SCALE, accum_out=den[:, h:h + 1])
                ins.then_inc(s_exp, 1)
                act.wait_ge(s_pt, 1)
                act.activation(pN[:, 0:8, :].rearrange("p a n -> p (a n)"), ps[0:TS, 2, :], ACT.Copy)
                act.activation(pN[:, 8:GH, :].rearrange("p a n -> p (a n)"), ps[0:TS, 3, 0:(GH - 8) * TS],
                               ACT.Copy).then_inc(s_pe, 1)
                act.wait_ge(s_used, 4 * NS)
                act.activation(oN[:], ps[0:TS, 4:4 + H, 0:P], ACT.Copy).then_inc(s_pe, 1)
                act.wait_ge(s_pt, 2)
                act.activation(k.oaT[:, :, SEQ:T], ps[:, 0, 0:H * TS].rearrange("p (h n) -> p h n", h=H),
                               ACT.Copy).then_inc(s_pe, 1)
                act.wait_ge(s_pe, 3)

            @block.vector
            def _(dve):
                chain = Chain(dve, s_chain)

                def lay(n, s, source):
                    if n >= NZ:
                        dve.wait_ge(s_used, 2 * (n - NZ + 1))
                    for g in range(G):
                        src = source(g)[:, :, s * LS:(s + 1) * LS].rearrange("p h (j r) -> p r h j", r=RES[g])
                        ins = dve.tensor_copy(places(n, g), src)
                    ins.then_inc(s_spread, 1)

                for n in range(NZ):
                    chain.step(dve.memset(spread[:, n, :], 0.0))
                    lay(n, n, lambda g: k.qkS[:, 2 * g * H:(2 * g + 1) * H, :])
                for s in range(NZ, NS):
                    lay(s, s, lambda g: k.qkS[:, 2 * g * H:(2 * g + 1) * H, :])
                dve.wait_ge(s_m, 16)
                dve.wait_ge(s_tr, 1)
                for g in range(G):
                    dve.tensor_tensor(sc[:, :, g, 0:P], ps[0:TS, 2 + g, :].rearrange("p (h n) -> p h n", h=H),
                                      broadcast_mid(smask[:, g, 0:P], H, 1), ALU.add)
                    b, o = 5 + (g * H) // 8, (g * H) % 8 * TS
                    ins = dve.tensor_tensor(sc[:, :, g, P:], ps[0:TS, b, o:o + H * TS].rearrange("p (h n) -> p h n", h=H),
                                            broadcast_mid(smask[:, g, P:], H, 1), ALU.add)
                chain.step(ins)
                v = sc[:].rearrange("p h g n -> p h (g n)")
                chain.step(dve.tensor_reduce(mx[:], v, AX, ALU.max))
                dve.tensor_scalar(nb[:], mx[:], -SCALE, None, ALU.mult).then_inc(s_nb, 1)
                dve.wait_ge(s_exp, 1)
                chain.step(dve.reciprocal(rden[:], den[:]))
                dve.tensor_tensor(v, v, broadcast_mid(rden[:], G * (P + TS), 2), ALU.mult).then_inc(s_norm, 1)
                dve.wait_ge(s_pt, 1)
                for s in range(NS):
                    lay(NS + s, s, lambda g: ps[:, g * H // 8, g * H % 8 * TS:(g * H % 8 + H) * TS].rearrange(
                        "p (h n) -> p h n", h=H))


def merge(nc, k, d, gate):
    with ExitStack() as ctx:
        wab = ctx.enter_context(nc.sbuf_tensor("mg_w", [P, 2, H, D], F32))
        s_w = [k.sem(f"mg_w{q}") for q in range(2)]
        s_sig, s_mm, s_t, s_add = (k.sem("mg_" + n) for n in ("sigmoid", "mm", "taken", "add"))
        ps = k.ps
        with nc.Block() as block:
            @block.sync
            def _(sp):
                for o in range(0, D, D // 2):
                    sp.dma_start(wab[:, 0, :, o:o + D // 2], d["w_a"][:, :, o:o + D // 2]).then_inc(s_w[2 * o // D], 16)
                    sp.dma_start(wab[:, 1, :, o:o + D // 2], d["w_b"][:, :, o:o + D // 2]).then_inc(s_w[2 * o // D], 16)

            @block.tensor
            def _(pe):
                for b in range(KD):
                    if b % (KD // 2) == 0:
                        pe.wait_ge(s_w[b // (KD // 2)], 32)
                    if b >= 2:
                        pe.wait_ge(s_t, 4 * (b - 1))
                    for br, src in ((0, k.hmT), (1, k.oaT)):
                        for c in range(H):
                            on = dict(start=c == 0, stop=c == H - 1)
                            wc = wab[:, br, c, b * P:(b + 1) * P]
                            pe.matmul(ps[:, 4 * (b % 2) + 2 * br, 0:TH], wc, src[:, c, 0:TH], **on)
                            mm = pe.matmul(ps[:, 4 * (b % 2) + 2 * br + 1, 0:TH], wc, src[:, c, TH:T], **on)
                    mm.then_inc(s_mm, 1)

            @block.scalar
            def _(act):
                for b in range(KD):
                    for br in range(2):
                        g = gate[:, br * KD + b, :]
                        act.activation(g, g, ACT.Sigmoid).then_inc(s_sig, 1)

            @block.vector
            def _(dve):
                for b in range(KD):
                    dve.wait_ge(s_sig, 2 * (b + 1))
                    dve.wait_ge(s_mm, b + 1)
                    for br in range(2):
                        g = gate[:, br * KD + b, :]
                        bank = 4 * (b % 2) + 2 * br
                        dve.tensor_tensor(g[:, 0:TH], ps[:, bank, 0:TH], g[:, 0:TH], ALU.mult).then_inc(s_t, 1)
                        dve.tensor_tensor(g[:, TH:T], ps[:, bank + 1, 0:TH], g[:, TH:T], ALU.mult).then_inc(s_t, 1)
                    dve.wait_ge(s_t, 4 * (b + 1))
                    dve.tensor_tensor(k.hT[:, b, :], gate[:, b, :], gate[:, KD + b, :], ALU.add).then_inc(s_add, 1)
                dve.wait_ge(s_add, KD)


def output_projection(nc, k, d, e):
    with ExitStack() as ctx:
        sb = lambda n, s, dt=F32: ctx.enter_context(nc.sbuf_tensor(n, s, dt))
        w = sb("op_w", [P, 2, KD, CHUNK])
        rows = sb("op_rows", [P, 2, 3, D])
        junk = sb("op_junk", [P, D])
        ss = sb("op_ss", [P, 2, NCH, 2])
        ms = sb("op_ms", [P, 2, NCH])
        rt = sb("op_rt", [P, 2, NCH])
        rs = sb("op_rs", [P, 2, NCH])
        y = sb("op_y", [P, 2, D])
        s_w = [k.sem(f"op_w{n}") for n in range(2)]
        s_r, s_x, s_mm, s_sq, s_ms, s_rt, s_y, s_x1, s_h2, s_tr, s_tt, s_chain, s_act, s_sc = (
            k.sem("op_" + n) for n in ("rows", "x", "mm", "square", "ms", "root", "taken", "x1", "h2", "turned",
                                       "turned_taken", "chain", "act", "scratch"))
        ps = k.ps
        with nc.Block() as block:
            @block.sync
            def _(sp):
                for n in range(2):
                    sp.dma_start(w[:, n], d["w_out"][n]).then_inc(s_w[n], 16)
                sp.dma_start(e.x1[:, 0:PT, :], d["x_prompt"].rearrange("(t p) n -> p t n", p=P)).then_inc(s_x, 16)
                sp.dma_start(e.x1[0:TS, PT, :], d["x_sample"]).then_inc(s_x, 16)
                for j in range(3):
                    sp.dma_start(rows[:, 0, j, :], d["rows"][j][0].partition_broadcast(P)).then_inc(s_r, 16)
                    for s in range(NS):
                        sp.dma_start(rows[s * LS:(s + 1) * LS, 1, j, :],
                                     d["rows"][j][1 + s].partition_broadcast(LS)).then_inc(s_r, 16)
                for n in range(e.wq.slots):
                    sp.dma_start(e.wq.w[:, n], d["peer_wq"][n]).then_inc(e.wq.ready[n], 16)
                e.wq.loaded = e.wq.slots

            @block.tensor
            def _(pe):
                def product(i):
                    r = tile_rows(i)
                    if i >= 2:
                        pe.wait_ge(s_y, i - 1)
                    for n in range(2):
                        if i == 0:
                            pe.wait_ge(s_w[n], 16)
                        for c in range(KD):
                            mm = pe.matmul(ps[0:r, 2 * (i % 2) + n, :], k.hT[:, c, tile_cols(i)], w[:, n, c, :],
                                           start=c == 0, stop=c == KD - 1)
                    mm.then_inc(s_mm, 1)

                def turn(i):
                    r = tile_rows(i)
                    pe.wait_ge(s_h2, i + 1)
                    if i >= 2:
                        pe.wait_ge(s_tt, i - 1)
                    for c in range(KD):
                        mm = pe.transpose(ps[:, 4 + 2 * (i % 2) + c // 4, (c % 4) * P:(c % 4) * P + r],
                                          e.h2[0:r, i, c * P:(c + 1) * P], k.ident[0:r, 0:r])
                    mm.then_inc(s_tr, 1)

                for i in range(NCH):
                    product(i)
                    if i >= 1:
                        turn(i - 1)
                turn(NCH - 1)

            @block.scalar
            def _(act):
                chain = Chain(act, s_act)
                for i in range(NCH):
                    r = tile_rows(i)
                    act.wait_ge(s_mm, i + 1)
                    for n in range(2):
                        chain.step(act.activation(junk[0:r, 0:CHUNK], ps[0:r, 2 * (i % 2) + n, :], ACT.Square,
                                                  accum_out=ss[0:r, 0, i, n:n + 1]))
                    act.sem_inc(s_sq, 1)
                    act.wait_ge(s_ms, 2 * i + 1)
                    act.activation(rt[0:r, 0, i:i + 1], ms[0:r, 0, i:i + 1], ACT.Sqrt).then_inc(s_rt, 1)
                    act.wait_ge(s_x1, i + 1)
                    act.activation(junk[0:r], e.x1[0:r, i, :], ACT.Square, accum_out=ss[0:r, 1, i, 0:1]).then_inc(s_sq, 1)
                    act.wait_ge(s_ms, 2 * i + 2)
                    act.activation(rt[0:r, 1, i:i + 1], ms[0:r, 1, i:i + 1], ACT.Sqrt).then_inc(s_rt, 1)
                    act.wait_ge(s_tr, i + 1)
                    src = ps[:, 4 + 2 * (i % 2):6 + 2 * (i % 2), :].rearrange("p b (c t) -> p (b c) t", t=P)
                    act.activation(e.h2T[:, :, tile_cols(i)], src[:, :, 0:r], ACT.Copy).then_inc(s_tt, 1)
                act.wait_ge(s_tt, NCH)

            @block.vector
            def _(dve):
                chain = Chain(dve, s_chain)
                dve.wait_ge(s_x, 32)
                dve.wait_ge(s_r, 16 * 3 * (1 + NS))
                for i in range(NCH):
                    r, kind = tile_rows(i), int(i == PT)
                    dve.wait_ge(s_sq, 2 * i + 1)
                    chain.step(dve.tensor_tensor(ss[0:r, 0, i, 0:1], ss[0:r, 0, i, 0:1], ss[0:r, 0, i, 1:2], ALU.add))
                    dve.tensor_scalar(ms[0:r, 0, i:i + 1], ss[0:r, 0, i, 0:1], 1.0 / D, EPS, ALU.mult,
                                      ALU.add).then_inc(s_ms, 1)
                    dve.wait_ge(s_rt, 2 * i + 1)
                    chain.step(dve.reciprocal(rs[0:r, 0, i:i + 1], rt[0:r, 0, i:i + 1]))
                    for n in range(2):
                        o = slice(n * CHUNK, (n + 1) * CHUNK)
                        ins = dve.scalar_tensor_tensor(y[0:r, 0, o], ps[0:r, 2 * (i % 2) + n, :], rs[0:r, 0, i:i + 1],
                                                       rows[0:r, kind, 0, o], ALU.mult, ALU.mult)
                    ins.then_inc(s_y, 1)
                    dve.wait_ge(s_y, i + 1)
                    dve.tensor_tensor(e.x1[0:r, i, :], e.x1[0:r, i, :], y[0:r, 0, :], ALU.add).then_inc(s_x1, 1)
                    dve.wait_ge(s_sq, 2 * i + 2)
                    dve.tensor_scalar(ms[0:r, 1, i:i + 1], ss[0:r, 1, i, 0:1], 1.0 / D, EPS, ALU.mult,
                                      ALU.add).then_inc(s_ms, 1)
                    dve.wait_ge(s_rt, 2 * i + 2)
                    chain.step(dve.reciprocal(rs[0:r, 1, i:i + 1], rt[0:r, 1, i:i + 1]))
                    chain.step(dve.scalar_tensor_tensor(y[0:r, 1, :], e.x1[0:r, i, :], rs[0:r, 1, i:i + 1],
                                                        rows[0:r, kind, 1, :], ALU.mult, ALU.mult))
                    dve.tensor_tensor(e.h2[0:r, i, :], y[0:r, 1, :], rows[0:r, kind, 2, :], ALU.add).then_inc(s_h2, 1)


def query_projections(nc, k, d, e):
    def take(n):
        def f(act, j, halves):
            act.activation(e.qT[:, H * n + j, 0:TH], halves[0], ACT.Copy)
            return act.activation(e.qT[:, H * n + j, TH:T], halves[1], ACT.Copy)
        return f
    project(nc, k, "qp", e.h2T, [("feature", d["peer_wq"][n], take(n)) for n in range(4)], e.wq)


def routed_beside(i, h):
    out = [(0, h + 1)] if i == 0 and h + 1 < PH else []
    if i + 1 < NCH and h < heads_of(i + 1):
        out.append((i + 1, h))
    return out


def routed_at(i, q):
    pairs = routed_beside(i, q // TOPK)
    if q % TOPK == 0:
        return pairs[:1] if len(pairs) == 2 else []
    return pairs[-1:] if q % TOPK == TOPK // 2 else []


ROUTED = [(0, 0)] + [x for i in range(NCH) for h in range(heads_of(i)) for x in routed_beside(i, h)]
RING = 10
FINISH = 4
BATCH = 2


def peer(nc, k, d, e):
    with ExitStack() as ctx:
        sb = lambda n, s, dt=F32: ctx.enter_context(nc.sbuf_tensor(n, s, dt))
        ring = sb("pr_ring", [P, RING, 2 * D])
        keysT = sb("pr_keysT", [P, 2, NKEYS])
        sc = sb("pr_sc", [P, 2, 2 * PH, NKEYS])
        packed = sb("pr_packed", [P, PH, P])
        rest = sb("pr_rest", [P, NKEYS])
        val = sb("pr_val", [P, 2, TOPK])
        ind = sb("pr_ind", [P, 2, TOPK], U32)
        indf = sb("pr_indf", [P, 2, TOPK])
        cand = sb("pr_cand", [P, TOPK, TOPK])
        crest = sb("pr_crest", [P, TOPK, TOPK])
        top = sb("pr_top", [P, TOPK])
        pos = sb("pr_pos", [P, TOPK], U32)
        part = sb("pr_part", [P, 2, TOPK], U32)
        partf = sb("pr_partf", [P, 2, TOPK])
        hot = sb("pr_hot", [P, 2, TOPK, TOPK])
        pick = sb("pr_pick", [P, 2, TOPK])
        ntop = sb("pr_ntop", [P, 1])
        ex = sb("pr_ex", [P, TOPK])
        exs = sb("pr_exs", [P, 1])
        rex = sb("pr_rex", [P, 1])
        idx = sb("pr_idx", [P, 2, SLOTS], U32)
        wgt = sb("pr_wgt", [P, 2, SLOTS])
        dots = sb("pr_dots", [P, RING])
        gel = sb("pr_gel", [P, RING])
        diag = sb("pr_diag", [P, RING, P])
        gate2 = sb("pr_gate2", [P, 2, D])
        fj = sb("pr_fj", [P, CHUNK])
        fy = sb("pr_fy", [P, D])
        fss = sb("pr_fss", [P, 2])
        fms = sb("pr_fms", [P, 1])
        frt = sb("pr_frt", [P, 1])
        frs = sb("pr_frs", [P, 1])
        arrived = [k.sem(f"pr_row{r}") for r in range(RING)]
        s_pk, s_keys, s_in, s_sc, s_sct, s_nt, s_ex, s_idx, s_dot, s_gel, s_dg, s_v, s_f, s_fsq, s_fms, s_frt, s_ft, s_y, s_out, s_chain, s_act = (
            k.sem("pr_" + n) for n in ("packed", "keys", "in", "scores", "scores_taken", "top", "exp", "routed", "dots", "gelu", "diag",
                                       "values", "sum", "sum_square", "sum_ms", "sum_root", "sum_taken", "y", "out",
                                       "chain", "act"))
        ps = k.ps
        order = list(range(NCH))
        routed = {x: n + 1 for n, x in enumerate(ROUTED)}
        with nc.Block() as block:
            @block.sync
            def _(sp):
                sp.dma_start(keysT[:], d["keysT"]).then_inc(s_keys, 16)
                sp.dma_start(e.h2[TS:P, PT, :], e.h2[0:TS, PT, :]).then_inc(s_in, 16)
                sp.dma_start(gate2[:, 0, :], d["rows"][3][0].partition_broadcast(P)).then_inc(s_in, 16)
                for s in range(NS):
                    sp.dma_start(gate2[s * LS:(s + 1) * LS, 1, :],
                                 d["rows"][3][1 + s].partition_broadcast(LS)).then_inc(s_in, 16)
                for i in order:
                    sp.wait_ge(s_y, i + 1)
                    if i < PT:
                        sp.dma_start(d["y_p"][i * P:(i + 1) * P, :], e.x1[:, i, :]).then_inc(s_out, 16)
                    else:
                        sp.dma_start(d["y_s"], e.x1[0:TS, i, :]).then_inc(s_out, 16)
                sp.wait_ge(s_out, 16 * NCH)
                sp.wait_ge(k.s_roll, 16 * k.n_rolls)

            @block.gpsimd
            def _(pool):
                for half in range(2):
                    ins = pool.tensor_copy(packed[:, :, half * TS:(half + 1) * TS],
                                           e.qT[:, half * PH:(half + 1) * PH, SEQ:T])
                ins.then_inc(s_pk, 1)
                for i in order:
                    for q in range(heads_of(i) * TOPK):
                        n = i * SLOTS + q
                        if q % TOPK == 0:
                            pool.wait_ge(s_idx, routed[i, q // TOPK])
                        if n >= RING:
                            pool.wait_ge(s_v, n - RING + 1)
                        pool.indirect_dma_start(ring[:, n % RING, :], None, d["uv"],
                                                bass.IndirectOffsetOnAxis(ap=idx[:, i % 2, q:q + 1], axis=0)
                                                ).then_inc(arrived[n % RING], 16)

            @block.tensor
            def _(pe):
                def scores(i):
                    if i >= 1:
                        pe.wait_ge(s_sct, i)
                    for b in range(2 * heads_of(i)):
                        q = e.qT[:, b, tile_cols(i)] if i < PT else packed[:, b, :]
                        mm = pe.matmul(ps[:, b // 4, (b % 4) * P:(b % 4 + 1) * P], q,
                                       keysT[:, b % 2, :], start=True, stop=True)
                    mm.then_inc(s_sc, 1)

                pe.wait_ge(s_keys, 16)
                scores(0)
                pe.wait_ge(s_pk, 1)
                for i in order:
                    r = tile_rows(i)
                    if i + 1 < NCH:
                        scores(i + 1)
                    if i >= 2:
                        pe.wait_ge(s_ft, i - 1)
                    last = heads_of(i) * TOPK - 1
                    for q in range(last + 1):
                        n = i * SLOTS + q
                        pe.wait_ge(s_dg, n + 1)
                        for half in range(2):
                            o = D + half * CHUNK
                            mm = pe.matmul(ps[0:r, 4 + 2 * (i % 2) + half, :], diag[:, n % RING, 0:r],
                                           ring[:, n % RING, o:o + CHUNK], start=q == 0, stop=q == last)
                        mm.then_inc(s_v, 1)

            @block.scalar
            def _(act):
                chain = Chain(act, s_act)

                def scores_taken(i):
                    act.wait_ge(s_sc, i + 1)
                    if i >= 2:
                        act.wait_ge(s_idx, routed[i - 2, PH - 1])
                    for b in range(heads_of(i) // 2):
                        ins = act.activation(sc[:, i % 2, 4 * b:4 * b + 4, :].rearrange("p a n -> p (a n)"),
                                             ps[:, b, :], ACT.Copy)
                    ins.then_inc(s_sct, 1)

                def route_exp(i, h):
                    act.wait_ge(s_nt, routed[i, h])
                    act.activation(ex[:], top[:], ACT.Exp, bias=ntop[:], accum_out=exs[:]).then_inc(s_ex, 1)

                def finish(i):
                    r = tile_rows(i)
                    act.wait_ge(s_v, i * SLOTS + heads_of(i) * TOPK)
                    if i >= 1:
                        act.wait_ge(s_y, i)
                    for half in range(2):
                        chain.step(act.activation(fj[0:r, 0:CHUNK], ps[0:r, 4 + 2 * (i % 2) + half, :], ACT.Square,
                                                  accum_out=fss[0:r, half:half + 1]))
                    act.sem_inc(s_fsq, 1)
                    act.wait_ge(s_fms, i + 1)
                    act.activation(frt[0:r], fms[0:r], ACT.Sqrt).then_inc(s_frt, 1)

                scores_taken(0)
                route_exp(0, 0)
                for i in order:
                    for h in range(heads_of(i)):
                        for q in range(h * TOPK, (h + 1) * TOPK, BATCH):
                            if i and q == FINISH:
                                finish(i - 1)
                            for t, g in routed_at(i, q):
                                if g == 0:
                                    scores_taken(t)
                                route_exp(t, g)
                            n = i * SLOTS + q
                            o = n % RING
                            act.wait_ge(s_dot, n // BATCH + 1)
                            act.activation(gel[:, o:o + BATCH], dots[:, o:o + BATCH], ACT.Gelu).then_inc(s_gel, 1)
                finish(NCH - 1)

            @block.vector
            def _(dve):
                chain = Chain(dve, s_chain)

                def top16(r, values, rest_, out, index):
                    chain.step(dve.max(out[0:r, 0:8], values))
                    dve.max_index(index[0:r, 0:8], out[0:r, 0:8], values)
                    chain.step(dve.match_replace(rest_, out[0:r, 0:8], values, NEG))
                    chain.step(dve.max(out[0:r, 8:16], rest_))
                    return dve.max_index(index[0:r, 8:16], out[0:r, 8:16], rest_)

                def route(i, h):
                    r, buf = P, i % 2
                    if h == 0:
                        dve.wait_ge(s_sct, i + 1)
                        if i >= 2:
                            dve.wait_ge(s_v, (i - 1) * SLOTS)
                    for half in range(2):
                        chain.step(top16(r, sc[:, i % 2, 2 * h + half, :], rest[:], val[:, half, :], ind[:, half, :]))
                    dve.tensor_copy(indf[0:r], ind[0:r])
                    chain.step(dve.tensor_tensor(cand[0:r], broadcast_mid(val[0:r, 0, :], TOPK, 2),
                                                 broadcast_mid(val[0:r, 1, :], TOPK, 1), ALU.add))
                    flat = cand[0:r].rearrange("p a b -> p (a b)")
                    chain.step(top16(r, flat, crest[0:r].rearrange("p a b -> p (a b)"), top[:], pos[:]))
                    dve.tensor_scalar(ntop[0:r], top[0:r, 0:1], -1.0, None, ALU.mult).then_inc(s_nt, 1)
                    dve.tensor_scalar(part[0:r, 0, :], pos[0:r], 4, None, ALU.logical_shift_right)
                    chain.step(dve.tensor_scalar(part[0:r, 1, :], pos[0:r], TOPK - 1, None, ALU.bitwise_and))
                    chain.step(dve.tensor_copy(partf[0:r], part[0:r]))
                    for half in range(2):
                        ins = dve.tensor_tensor(hot[0:r, half], broadcast_mid(partf[0:r, half, :], TOPK, 2),
                                                broadcast_mid(k.iota[0:r], TOPK, 1), ALU.is_equal)
                    chain.step(ins)
                    for half in range(2):
                        ins = dve.tensor_tensor(hot[0:r, half], hot[0:r, half],
                                                broadcast_mid(indf[0:r, half, :], TOPK, 1), ALU.mult)
                    chain.step(ins)
                    chain.step(dve.tensor_reduce(pick[0:r], hot[0:r], AX, ALU.add))
                    o = slice(h * TOPK, (h + 1) * TOPK)
                    dve.scalar_tensor_tensor(idx[0:r, buf, o], pick[0:r, 0, :], float(NKEYS), pick[0:r, 1, :],
                                             ALU.mult, ALU.add)
                    dve.wait_ge(s_ex, routed[i, h])
                    chain.step(dve.reciprocal(rex[0:r], exs[0:r]))
                    dve.tensor_scalar(wgt[0:r, buf, o], ex[0:r], rex[0:r], None, ALU.mult).then_inc(s_idx, 1)
                    dve.wait_ge(s_idx, routed[i, h])

                def dots_of(i, q):
                    for b in range(BATCH):
                        n = i * SLOTS + q + b
                        dve.wait_ge(arrived[n % RING], 16 * (n // RING + 1))
                        u = ring[:, n % RING, 0:D]
                        ins = dve.tensor_tensor_reduce(u, u, e.h2[:, i, :], 1.0, 0.0, ALU.mult, ALU.add,
                                                       dots[:, n % RING:n % RING + 1])
                        if b == BATCH - 1:
                            ins.then_inc(s_dot, 1)

                def diags_of(i, q):
                    r = tile_rows(i)
                    n = i * SLOTS + q
                    dve.wait_ge(s_gel, n // BATCH + 1)
                    for b in range(BATCH):
                        o = (n + b) % RING
                        dve.tensor_scalar(diag[:, o, 0:r], k.ident[:] if i < PT else k.fold[:], gel[:, o:o + 1],
                                          wgt[:, i % 2, q + b:q + b + 1], ALU.mult, ALU.mult).then_inc(s_dg, 1)

                def finish(i):
                    r, kind = tile_rows(i), int(i == PT)
                    dve.wait_ge(s_fsq, i + 1)
                    chain.step(dve.tensor_tensor(fss[0:r, 0:1], fss[0:r, 0:1], fss[0:r, 1:2], ALU.add))
                    dve.tensor_scalar(fms[0:r], fss[0:r, 0:1], 1.0 / D, EPS, ALU.mult, ALU.add).then_inc(s_fms, 1)
                    dve.wait_ge(s_frt, i + 1)
                    chain.step(dve.reciprocal(frs[0:r], frt[0:r]))
                    for half in range(2):
                        o = slice(half * CHUNK, (half + 1) * CHUNK)
                        ins = dve.scalar_tensor_tensor(fy[0:r, o], ps[0:r, 4 + 2 * (i % 2) + half, :], frs[0:r],
                                                       gate2[0:r, kind, o], ALU.mult, ALU.mult)
                    ins.then_inc(s_ft, 1)
                    dve.wait_ge(s_ft, i + 1)
                    dve.tensor_tensor(e.x1[0:r, i, :], e.x1[0:r, i, :], fy[0:r], ALU.add).then_inc(s_y, 1)

                route(0, 0)
                dve.wait_ge(s_in, 16 * (2 + NS))
                for i in order:
                    for h in range(heads_of(i)):
                        for q in range(h * TOPK, (h + 1) * TOPK, BATCH):
                            if i and q == FINISH:
                                finish(i - 1)
                            for t, g in routed_at(i, q):
                                route(t, g)
                            dots_of(i, q)
                            if q:
                                diags_of(i, q - BATCH)
                            elif i:
                                diags_of(i - 1, heads_of(i - 1) * TOPK - BATCH)
                diags_of(NCH - 1, heads_of(NCH - 1) * TOPK - BATCH)
                finish(NCH - 1)


def build(nc, d):
    with ExitStack() as ctx:
        sb = lambda n, s, dt=F32, c=ctx: c.enter_context(nc.sbuf_tensor(n, s, dt))
        k = Shared()
        k.sem = lambda n: ctx.enter_context(nc.semaphore(n))
        k.ps = ctx.enter_context(nc.psum_tensor("ps", [P, 8, 512], F32))
        k.ident = sb("ident", [P, P])
        k.sel = sb("sel", [H, H * P])
        k.block = sb("block", [TS, NS])
        k.fold = sb("fold", [P, TS])
        k.iota = sb("iota", [P, TOPK])
        k.shift1 = sb("shift1", [P, KD, NC])
        k.scale1 = sb("scale1", [P, KD, NC])
        k.s_roll = k.sem("rolled")
        k.rolls = roll_pieces(d)
        k.n_rolls = len(k.rolls)
        trunk = sb("trunk", [P, 2 * KD, T])
        k.hT, k.oaT, k.hmT = trunk[:, 0:KD, :], trunk[:, KD:KD + H, :], trunk[:, KD + H:, :]
        with ExitStack() as first:
            n = Shared()
            n.x, n.ss = sb("x_rows", [P, NCH, D], F32, first), sb("x_ss", [P, NCH], F32, first)
            modulation(nc, k, d, n)
            normalised_input(nc, k, d, n)
        with ExitStack() as att:
            k.qkS = sb("qkS", [P, 2 * G * H, TS], F32, att)
            k.vS = sb("vS", [TS, G, H * P], F32, att)
            with ExitStack() as pa:
                a = Shared()
                a.qk = sb("a_qk", [P, 2 * G * H, SEQ], F32, pa)
                a.v = sb("a_v", [P, PT, G, H * P], F32, pa)
                attention_projections(nc, k, d, a)
                prompt_attention(nc, k, d, a)
            sample_attention(nc, k, d)
        with ExitStack() as mg:
            gates = MergeGates(nc, k, d, mg)
            with ExitStack() as ml:
                ms = lambda n, s: sb(n, s, F32, ml)
                m = Shared()
                m.raw, m.rawS = ms("m_raw", [P, 2 * H, CW - 1 + SEQ]), ms("m_rawS", [P, 2 * H, NS * (CW - 1 + LS)])
                m.v, m.o, m.qk = ms("m_v", [P, NCH, H * P]), ms("m_o", [P, NCH, H * P]), ms("m_qk", [P, 2 * H, T])
                m.rows, m.M, m.decay = ms("m_rows", [H, 4, T]), ms("m_M", [H, T]), ms("m_decay", [H, PT + NS])
                m.cols, m.dcols, m.ones = ms("m_cols", [P, NCH, 4, H]), ms("m_dcols", [P, H, PT + NS]), ms("m_ones", [P, 1])
                mlstm_projections(nc, k, d, m)
                gates.allocate_ring(nc, ml)
                conv_and_gates(nc, k, d, m, gates)
                mlstm(nc, k, d, m, gates)
            merge(nc, k, d, gates.gate)
        e = Shared()
        e.x1, e.h2, e.qT = sb("x1", [P, NCH, D]), sb("h2", [P, NCH, D]), trunk
        with ExitStack() as mid:
            e.h2T = sb("h2T", [P, KD, T], F32, mid)
            e.wq = weight_ring(nc, k, "qp", mid, 2)
            output_projection(nc, k, d, e)
            query_projections(nc, k, d, e)
        peer(nc, k, d, e)


def kernel(**inputs):
    import concourse.bacc as bacc
    from concourse.bass_utils import run_bass_kernel_spmd

    a = {n: np.asarray(x) for n, x in inputs.items()}
    W = H * P
    w_in = a["w_in"][0]
    at = np.cumsum([0, 2 * W, W, W, H, H] + [W] * (3 * G) + [D, D]).tolist()

    def by_row(w):
        return w.reshape(-1, P, w.shape[1]).transpose(1, 0, 2)

    def chunks(w):
        return np.stack([by_row(w[:, o:o + CHUNK]) for o in range(0, w.shape[1], CHUNK)])

    def part(i, n=1):
        return w_in[:, at[i]:at[i + n]]

    attn = [part(5 + 3 * g + j) for g in range(G) for j in range(2)]
    ins = {
        "cT": by_row(np.concatenate([a["c_prompt"], a["c_sample"]]).T),
        "w_ada": chunks(a["w_ada"][0]), "b_ada": a["b_ada"][0],
        "g_pre1": a["g_pre1"][0].reshape(KD, P).T, "g_post1": a["g_post1"][0], "g_pre2": a["g_pre2"][0],
        "g_post2": a["g_post2"][0],
        "x_prompt": a["x_prompt"][0], "x_sample": a["x_sample"].reshape(TS, D),
        "w_attn_qk": np.stack([by_row(w) for w in attn]),
        "w_attn_v": np.stack([by_row(part(7 + 3 * g)) for g in range(G)]),
        "w_qk": chunks(part(0)), "w_mv": by_row(part(1)), "w_mo": by_row(part(2)),
        "w_gates": by_row(part(3, 2)), "b_gates": np.stack([a["b_igate"][0], a["b_fgate"][0]], 1),
        "w_merge": np.stack([by_row(part(14, 2)[:, o:o + P]) for o in range(0, 2 * D, P)]),
        "conv_w": np.concatenate([a["conv_w"][0], a["conv_b"]]).reshape(CW + 1, 2 * H, P).transpose(2, 1, 0),
        "stateT": a["state_conv"][0].reshape(NS, CW - 1, 2 * H, P).transpose(3, 2, 0, 1),
        "m0": a["state_mlstm_m"][0].T,
        "C0": a["state_mlstm_C"][0].transpose(2, 0, 1, 3), "n0": a["state_mlstm_n"][0].transpose(2, 0, 1),
        "mh_norm_g": a["mh_norm_g"][0].reshape(H, P).T,
        "w_a": by_row(a["w_a"][0]), "w_b": by_row(a["w_b"][0]), "w_out": chunks(a["w_out"][0]),
        "peer_wq": chunks(a["peer_wq"][0]),
        "keysT": np.stack([a["peer_k1"][0].T, a["peer_k2"][0].T], 1),
        "uv": np.concatenate([a["peer_u"][0], a["peer_v"][0]], 1),
    }
    kc = []
    for g in range(G):
        c = a[f"cache_win{g}_kv"][0]
        ins[f"cache{g}"] = c.reshape(NS, -1)
        keys = c[:, :, 0].reshape(NS, P, DILATIONS[g], H, P)[:, :, :RES[g]]
        kc.append(keys.transpose(0, 4, 2, 3, 1).reshape(NS, P, -1))
    ins["kcacheA"] = np.concatenate(kc[:2], 2)
    ins["kcacheB"] = kc[2]
    ins.update(constants())
    ins = {n: np.ascontiguousarray(x) for n, x in ins.items()}
    outs = {
        "y_p": (SEQ, D), "y_s": (TS, D), "kT_p": (G, P, H, SEQ), "v_p": (G, P, PT, W), "kT_s": (G, P, H, TS),
        "v_s": (TS, G, W), "C_p": (P, H, P), "n_p": (P, H), "C_s": (P, NS, H, P), "n_s": (P, NS, H),
        "m_new": (H, 1 + NS), "conv_p": (P, 2 * H, CW - 1), "conv_s": (P, 2 * H, NS, CW - 1),
        **{f"win{g}_s": (NS, (WINDOWS[g] - LS) * D) for g in range(G)},
    }
    nc = bacc.Bacc("TRN2", target_bir_lowering=False, num_devices=1)
    d = {n: nc.dram_tensor("in_" + n, x.shape, mybir.dt.from_np(x.dtype), kind="ExternalInput").ap()
         for n, x in ins.items()}
    d.update({n: nc.dram_tensor("out_" + n, s, F32, kind="ExternalOutput").ap() for n, s in outs.items()})
    d["rows"] = nc.dram_tensor("rows", (4, NC, D), F32, kind="Internal").ap()
    build(nc, d)
    res = run_bass_kernel_spmd(nc, [{"in_" + n: x for n, x in ins.items()}], core_ids=[0]).results[0]
    r = {n: np.asarray(res["out_" + n]).reshape(s) for n, s in outs.items()}

    win_p, win_s = [], []
    for g in range(G):
        keys = r["kT_p"][g].transpose(2, 1, 0)
        vals = r["v_p"][g].transpose(1, 0, 2).reshape(SEQ, H, P)
        keep = min(WINDOWS[g], SEQ)
        win_p.append(np.stack([keys, vals], 1)[SEQ - keep:][None, None])
        nk = r["kT_s"][g].transpose(2, 1, 0).reshape(NS, LS, H, P)
        nv = r["v_s"][:, g].reshape(NS, LS, H, P)
        old = r[f"win{g}_s"].reshape(NS, WINDOWS[g] - LS, 2, H, P)
        win_s.append(np.concatenate([old, np.stack([nk, nv], 2)], 1)[None])
    C_s = r["C_s"].transpose(1, 2, 0, 3)[None]
    return (r["y_p"][None], r["y_s"].reshape(NS, LS, D), *win_p,
            r["C_p"].transpose(1, 0, 2)[None, None], r["n_p"].T[None, None], r["m_new"][:, 0][None, None],
            r["conv_p"].transpose(2, 1, 0).reshape(1, 1, CW - 1, 2 * W), *win_s,
            C_s, r["n_s"].transpose(1, 2, 0)[None], r["m_new"][:, 1:].T[None],
            r["conv_s"].transpose(2, 3, 1, 0).reshape(1, NS, CW - 1, 2 * W))
```
